# Optimizing a Trainium2 kernel written in Bass

```python
import jax, jax.numpy as jnp
from jax import lax
import numpy as np

D_MODEL = 1024
BATCH = 1
SEQ = 512
DEPTH = 2
DEC_BATCH = 1
DEC_SEQ = 64
PAST_LEN = 512

CHUNK = 64
NORM_EPS = 1e-6
GLA_HEADS = 4
GLA_DV = D_MODEL // 2 // GLA_HEADS
GLA_DK = GLA_DV // 2
GLA_K = GLA_HEADS * GLA_DK
GLA_V = GLA_HEADS * GLA_DV
GLA_LR = 16
GLA_GATE_NORMALIZER = 16.0
RWKV_N = 64
RWKV_C = D_MODEL // 2
RWKV_HEADS = RWKV_C // RWKV_N
RWKV_W_LR = 64
RWKV_A_LR = 64
RWKV_G_LR = 128
RWKV_GN_EPS = 64e-5
GLA_COLS = 2 * GLA_K + 2 * GLA_V + GLA_LR
RWKV_COLS = 3 * RWKV_C + RWKV_W_LR + RWKV_A_LR + RWKV_G_LR
IN_COLS = GLA_COLS + RWKV_COLS
MIX_WIDTH = GLA_V + RWKV_C
D_FF = 2816
CONV_W = 3

kernel_name = 'hymba_gla_rwkv7_convffn_stream_step'

def _split(x, sizes):
    idx = [int(i) for i in np.cumsum(sizes)[:-1]]
    return jnp.split(x, idx, axis=-1)

def _rmsnorm(x, g):
    xf = x.astype(jnp.float32)
    y = xf * lax.rsqrt(jnp.mean(xf * xf, axis=-1, keepdims=True) + NORM_EPS)
    return (y * g.astype(jnp.float32)).astype(x.dtype)

def _gla_chunked(q, k, v, log_a, s0):
    b_, l_, h_, _ = q.shape
    dv = v.shape[-1]
    c = min(CHUNK, l_)
    n = l_ // c

    def to_blocks(t):
        return t.reshape(b_, n, c, h_, t.shape[-1]).transpose(1, 0, 3, 2, 4)

    causal = jnp.tril(jnp.ones((c, c), dtype=bool))

    def step(s, inp):
        qc, kc, vc, lac = inp
        cum = jnp.cumsum(lac, axis=2)
        last = cum[:, :, -1:, :]
        q_e = qc * jnp.exp(cum)
        k_e = kc * jnp.exp(-cum)
        scores = jnp.where(causal, jnp.einsum('bhtk,bhsk->bhts', q_e, k_e), 0.0)
        o = jnp.einsum('bhts,bhsv->bhtv', scores, vc) + jnp.einsum('bhtk,bhkv->bhtv', q_e, s)
        s_new = s * jnp.exp(last[:, :, 0, :])[..., None] + jnp.einsum(
            'bhsk,bhsv->bhkv', kc * jnp.exp(last - cum), vc)
        return s_new, o

    s_fin, o = lax.scan(step, s0, (to_blocks(q), to_blocks(k), to_blocks(v), to_blocks(log_a)))
    o = o.transpose(1, 0, 3, 2, 4).reshape(b_, l_, h_, dv)
    return o, s_fin

def _rwkv7_scan(r, w, k, v, a_vec, b_vec, s0):
    def step(s, inp):
        rt, wt, kt, vt, at, bt = inp
        sa = jnp.einsum('bhvk,bhk->bhv', s, at)
        s = s * wt[:, :, None, :] + sa[..., None] * bt[:, :, None, :] + vt[..., None] * kt[:, :, None, :]
        y = jnp.einsum('bhvk,bhk->bhv', s, rt)
        return s, y

    xs = tuple(t.transpose(1, 0, 2, 3) for t in (r, w, k, v, a_vec, b_vec))
    s_fin, y = lax.scan(step, s0, xs)
    return y.transpose(1, 0, 2, 3), s_fin

def _token_mixers(h, s_gla, s_rwkv, shift_prev, p, l):
    f32 = jnp.float32
    bsz, seq, _ = h.shape
    proj = jnp.einsum('bld,dc->blc', h, p['w_in'][l])
    p_gla, p_rwkv = proj[..., :GLA_COLS], proj[..., GLA_COLS:]

    gq, gk, gv, gg, glr = _split(p_gla, (GLA_K, GLA_K, GLA_V, GLA_V, GLA_LR))
    q = gq.astype(f32).reshape(bsz, seq, GLA_HEADS, GLA_DK) * (GLA_DK ** -0.5)
    k = gk.astype(f32).reshape(bsz, seq, GLA_HEADS, GLA_DK)
    v = gv.astype(f32).reshape(bsz, seq, GLA_HEADS, GLA_DV)
    gate_logit = (glr @ p['gla_gate_w2'][l] + p['gla_gate_b'][l]).astype(f32)
    log_a = (jax.nn.log_sigmoid(gate_logit) / GLA_GATE_NORMALIZER).reshape(bsz, seq, GLA_HEADS, GLA_DK)
    o_gla, s_gla_new = _gla_chunked(q, k, v, log_a, s_gla.astype(f32))
    o_gla = o_gla * lax.rsqrt(jnp.mean(o_gla * o_gla, axis=-1, keepdims=True) + NORM_EPS) * p['gla_norm_w'][l]
    o_gla = o_gla.reshape(bsz, seq, GLA_V) * jax.nn.silu(gg.astype(f32))

    prev = jnp.concatenate([shift_prev[:, None, :].astype(p_rwkv.dtype), p_rwkv[:, :-1]], axis=1)
    xs = p_rwkv + p['rwkv_mu'][l] * (prev - p_rwkv)
    shift_new = p_rwkv[:, -1]
    xr, xk, xv, xw, xa, xg = _split(xs, (RWKV_C, RWKV_C, RWKV_C, RWKV_W_LR, RWKV_A_LR, RWKV_G_LR))
    w_raw = (p['rwkv_w0'][l] + jnp.tanh(xw) @ p['rwkv_w2'][l]).astype(f32)
    w_log = -jnp.exp(-jax.nn.softplus(-w_raw) - 0.5)
    a = jax.nn.sigmoid((p['rwkv_a0'][l] + xa @ p['rwkv_a2'][l]).astype(f32))
    g = (jax.nn.sigmoid(xg) @ p['rwkv_g2'][l]).astype(f32)
    r = xr.astype(f32)
    kr = xk.astype(f32)
    vr = xv.astype(f32)
    kk = (kr * p['rwkv_k_k'][l]).reshape(bsz, seq, RWKV_HEADS, RWKV_N)
    kk = kk / jnp.maximum(jnp.sqrt(jnp.sum(kk * kk, axis=-1, keepdims=True)), 1e-12)
    kr = kr * (1.0 + (a - 1.0) * p['rwkv_k_a'][l])
    heads = lambda t: t.reshape(bsz, seq, RWKV_HEADS, RWKV_N)
    rh, kh, vh, ah = heads(r), heads(kr), heads(vr), heads(a)
    y, s_rwkv_new = _rwkv7_scan(rh, jnp.exp(heads(w_log)), kh, vh, -kk, kk * ah, s_rwkv.astype(f32))
    mu = jnp.mean(y, axis=-1, keepdims=True)
    var = jnp.mean(jnp.square(y - mu), axis=-1, keepdims=True)
    y = ((y - mu) * lax.rsqrt(var + RWKV_GN_EPS)).reshape(bsz, seq, RWKV_C)
    y = y * p['rwkv_ln_w'][l] + p['rwkv_ln_b'][l]
    bonus = jnp.sum(rh * kh * p['rwkv_r_k'][l], axis=-1, keepdims=True) * vh
    y = (y + bonus.reshape(bsz, seq, RWKV_C)) * g

    mixed = jnp.concatenate([o_gla, y], axis=-1).astype(h.dtype)
    out = jnp.einsum('blc,cd->bld', mixed, p['w_out'][l])
    return out, s_gla_new, s_rwkv_new, shift_new

def _conv_ffn(h, conv_prev, w_up, conv_w, conv_b, w_down):
    seq = h.shape[1]
    uv = jnp.einsum('bld,df->blf', h, w_up)
    u, gate = uv[..., :D_FF], uv[..., D_FF:]
    u_ext = jnp.concatenate([conv_prev.astype(u.dtype), u], axis=1)
    uc = conv_b + sum(conv_w[j] * u_ext[:, j:j + seq] for j in range(CONV_W))
    conv_new = u_ext[:, seq:]
    y = jnp.einsum('blf,fd->bld', jax.nn.gelu(uc, approximate=False) * gate, w_down)
    return y, conv_new

def _trunk(x, s_gla, s_rwkv, s_shift, c_conv, p):
    new_gla, new_rwkv, new_shift, new_conv = [], [], [], []
    for l in range(DEPTH):
        mix, sg, sr, ss = _token_mixers(_rmsnorm(x, p['norm_mix'][l]), s_gla[l], s_rwkv[l], s_shift[l], p, l)
        x = x + mix
        f, cc = _conv_ffn(_rmsnorm(x, p['norm_ffn'][l]), c_conv[l], p['ffn_w_up'][l], p['ffn_conv_w'][l],
                          p['ffn_conv_b'][l], p['ffn_w_down'][l])
        x = x + f
        new_gla.append(sg.astype(s_gla.dtype))
        new_rwkv.append(sr.astype(s_rwkv.dtype))
        new_shift.append(ss.astype(s_shift.dtype))
        new_conv.append(cc.astype(c_conv.dtype))
    y = _rmsnorm(x, p['norm_final'])
    return y, jnp.stack(new_gla), jnp.stack(new_rwkv), jnp.stack(new_shift), jnp.stack(new_conv)

def setup_inputs(seed: int = 0) -> dict:
    key = jax.random.key(seed)
    ks = jax.random.split(key, 30)
    f32 = jnp.float32

    def nrm(k, shape, s):
        return jax.random.normal(k, shape, f32) * s

    return {
        'x_prompt': nrm(ks[0], (BATCH, SEQ, D_MODEL), 1.0),
        'x_sample': nrm(ks[1], (DEC_BATCH, DEC_SEQ, D_MODEL), 1.0),
        'state_gla': nrm(ks[2], (DEPTH, DEC_BATCH, GLA_HEADS, GLA_DK, GLA_DV), 0.1),
        'state_rwkv': nrm(ks[3], (DEPTH, DEC_BATCH, RWKV_HEADS, RWKV_N, RWKV_N), 0.1),
        'state_rwkv_shift': nrm(ks[4], (DEPTH, DEC_BATCH, RWKV_COLS), 1.0),
        'cache_ffn_conv': nrm(ks[5], (DEPTH, DEC_BATCH, CONV_W - 1, D_FF), 1.0),
        'norm_mix': 1.0 + nrm(ks[6], (DEPTH, D_MODEL), 0.02),
        'w_in': nrm(ks[7], (DEPTH, D_MODEL, IN_COLS), D_MODEL ** -0.5),
        'gla_gate_w2': nrm(ks[8], (DEPTH, GLA_LR, GLA_K), GLA_LR ** -0.5),
        'gla_gate_b': nrm(ks[9], (DEPTH, GLA_K), 0.1),
        'gla_norm_w': 1.0 + nrm(ks[10], (DEPTH, GLA_DV), 0.02),
        'rwkv_mu': jax.random.uniform(ks[11], (DEPTH, RWKV_COLS), f32),
        'rwkv_w0': nrm(ks[12], (DEPTH, RWKV_C), 0.5),
        'rwkv_w2': nrm(ks[13], (DEPTH, RWKV_W_LR, RWKV_C), 0.1),
        'rwkv_a0': nrm(ks[14], (DEPTH, RWKV_C), 0.1),
        'rwkv_a2': nrm(ks[15], (DEPTH, RWKV_A_LR, RWKV_C), 0.1),
        'rwkv_g2': nrm(ks[16], (DEPTH, RWKV_G_LR, RWKV_C), RWKV_G_LR ** -0.5),
        'rwkv_k_k': 0.85 + nrm(ks[17], (DEPTH, RWKV_C), 0.05),
        'rwkv_k_a': 1.0 + nrm(ks[18], (DEPTH, RWKV_C), 0.05),
        'rwkv_r_k': nrm(ks[19], (DEPTH, RWKV_HEADS, RWKV_N), 0.1),
        'rwkv_ln_w': 1.0 + nrm(ks[20], (DEPTH, RWKV_C), 0.02),
        'rwkv_ln_b': nrm(ks[21], (DEPTH, RWKV_C), 0.01),
        'w_out': nrm(ks[22], (DEPTH, MIX_WIDTH, D_MODEL), MIX_WIDTH ** -0.5),
        'norm_ffn': 1.0 + nrm(ks[23], (DEPTH, D_MODEL), 0.02),
        'ffn_w_up': nrm(ks[24], (DEPTH, D_MODEL, 2 * D_FF), D_MODEL ** -0.5),
        'ffn_conv_w': nrm(ks[25], (DEPTH, CONV_W, D_FF), CONV_W ** -0.5),
        'ffn_conv_b': nrm(ks[26], (DEPTH, D_FF), 0.01),
        'ffn_w_down': nrm(ks[27], (DEPTH, D_FF, D_MODEL), D_FF ** -0.5),
        'norm_final': 1.0 + nrm(ks[28], (D_MODEL,), 0.02),
    }

def reference(x_prompt, x_sample, state_gla, state_rwkv, state_rwkv_shift, cache_ffn_conv,
              norm_mix, w_in, gla_gate_w2, gla_gate_b, gla_norm_w, rwkv_mu, rwkv_w0, rwkv_w2,
              rwkv_a0, rwkv_a2, rwkv_g2, rwkv_k_k, rwkv_k_a, rwkv_r_k, rwkv_ln_w, rwkv_ln_b,
              w_out, norm_ffn, ffn_w_up, ffn_conv_w, ffn_conv_b, ffn_w_down, norm_final):
    params = dict(norm_mix=norm_mix, w_in=w_in, gla_gate_w2=gla_gate_w2, gla_gate_b=gla_gate_b,
                  gla_norm_w=gla_norm_w, rwkv_mu=rwkv_mu, rwkv_w0=rwkv_w0, rwkv_w2=rwkv_w2,
                  rwkv_a0=rwkv_a0, rwkv_a2=rwkv_a2, rwkv_g2=rwkv_g2, rwkv_k_k=rwkv_k_k,
                  rwkv_k_a=rwkv_k_a, rwkv_r_k=rwkv_r_k, rwkv_ln_w=rwkv_ln_w, rwkv_ln_b=rwkv_ln_b,
                  w_out=w_out, norm_ffn=norm_ffn, ffn_w_up=ffn_w_up, ffn_conv_w=ffn_conv_w,
                  ffn_conv_b=ffn_conv_b, ffn_w_down=ffn_w_down, norm_final=norm_final)
    nb = x_prompt.shape[0]
    g0 = jnp.zeros((DEPTH, nb, GLA_HEADS, GLA_DK, GLA_DV), state_gla.dtype)
    r0 = jnp.zeros((DEPTH, nb, RWKV_HEADS, RWKV_N, RWKV_N), state_rwkv.dtype)
    sh0 = jnp.zeros((DEPTH, nb, RWKV_COLS), state_rwkv_shift.dtype)
    c0 = jnp.zeros((DEPTH, nb, CONV_W - 1, D_FF), cache_ffn_conv.dtype)
    y_prompt, gla_p, rwkv_p, shift_p, conv_p = _trunk(x_prompt, g0, r0, sh0, c0, params)
    y_sample, gla_s, rwkv_s, shift_s, conv_s = _trunk(
        x_sample, state_gla, state_rwkv, state_rwkv_shift, cache_ffn_conv, params)
    return (y_prompt, y_sample, gla_p, rwkv_p, shift_p, conv_p, gla_s, rwkv_s, shift_s, conv_s)


_drawn_inputs = setup_inputs


def setup_inputs(seed=0):
    import zlib

    import numpy as np

    out = dict(_drawn_inputs(seed))
    spreads = {}
    factors = {'gla_norm_w': 4.079,
     'rwkv_k_k': 14.052,
     'rwkv_ln_w': 5.299,
     'rwkv_ln_b': 21.455,
     'ffn_conv_b': 6.909,
     'norm_final': 7.498}
    for name, (base, spread) in spreads.items():
        noise = np.random.default_rng([zlib.crc32(name.encode()), seed]).standard_normal(out[name].shape)
        drawn = base * np.exp(spread * noise) if base else spread * noise
        out[name] = __import__('jax').numpy.asarray(drawn.astype(out[name].dtype))
    for name, factor in factors.items():
        out[name] = (out[name] * factor).astype(out[name].dtype)
    return out
```

```python
from contextlib import ExitStack

import concourse.bass as bass
from concourse import mybir

F32 = mybir.dt.float32
F32R = mybir.dt.float32r
BF16 = mybir.dt.bfloat16
ALU = mybir.AluOpType
ACT = mybir.ActivationFunctionType

P = 128
D = 1024
SEQ = 512
DEC = 64
DEPTH = 2
TOK = SEQ + DEC
C = 64
NCH = TOK // C
KT = D // P
GH, GDV = 4, 128
GDK = 64
GK, GV = GH * GDK, GH * GDV
RC, RN = 512, 64
NP = RC // P
GLA_COLS = 2 * GK + 2 * GV + 16
RWKV_COLS = 3 * RC + 256
IN_COLS = GLA_COLS + RWKV_COLS
RT = RWKV_COLS // P
GT = (2 * GK + 2 * GV) // P
LR_AT = 96
F = 2816
HALVES = 2
FT = F // P // HALVES
CP = C + 1
EPS = 1e-6
GN_EPS = 64e-5
KAPPA = 0.6065306597126334
LN2 = 0.6931471805599453

ROWS_A, ROWS_B = {}, {}
_n = 0
for _name, _count in (("norm_mix", 8), ("norm_ffn", 8), ("norm_final", 8), ("gate_b", 2), ("gla_w", 1),
                      ("mu", RT), ("w0", 4), ("a0", 4), ("k_k", 4), ("k_a", 4), ("r_k", 4),
                      ("ln_w", 4), ("ln_b", 4), ("shift", RT), ("cache", 44)):
    ROWS_A[_name] = (_n, _count)
    _n += _count
NA = _n
_n = 0
for _name, _count in (("conv_w", 66), ("conv_b", 22)):
    ROWS_B[_name] = (_n, _count)
    _n += _count
NB = _n

PAIRS = dict(rwkv=0, gla=RT // 2, out=RT // 2 + GT // 2, ffn=RT // 2 + GT // 2 + KT // 2)
FFN_PAIRS = FT + KT // 2
PAIRS_OF_LAYER = PAIRS["ffn"] + HALVES * FFN_PAIRS


N_ROWS = 17
A_TANH, A_W, A_A, A_SQ, A_LN, A_GE, N_PRE_ACT = 1, 3, 7, 11, 15, 23, 26
D_ZERO, D_KK, D_MAX, D_ABS, N_PRE_DVE = 2, 3, 11, 32, 38
N_PRE_PE = 14
F_STEPS = 8
R_STEPS = 4
N_CONSTS = 44


def turn(s, l, pair, after_lowrank=True):
    if s == 0:
        return l * (PAIRS_OF_LAYER + 1) + pair + (1 if after_lowrank else 0)
    return l * PAIRS_OF_LAYER + pair


PE_C = ["g_scores", "g_tok", "gramA", "gramB", "g_out", "g_state", "tokA", "tokB",
        "sq2A", "sq2B", "sq4A", "T2A", "sq4B", "T2B", "sq8A", "T4A", "sq8B", "T4B", "T8A", "T8B",
        "FA", "FB", "F2A", "F2B", "ZA", "ZB", "Z1A", "Z1B", "Z2A", "Z2B", "UA", "UB",
        "YA", "SA", "YB", "SB", "bonus"]
AC_C = ["P", "Pinv", "Eg", "Ei", "g_tok", "g_even", "g_odd", "tokA", "tokB", "sq2A", "sq2B",
        "sq4A", "sq4B", "sq8A", "sq8B", "FA", "FB", "F2A", "F2B", "ZA", "ZB", "Z1A", "Z1B", "YA", "YB"]
DV_C = ["qe", "ke", "at", "bt", "kt", "g_scores", "QA", "KA", "DA", "EA", "TA", "QB", "KB", "DB", "EB", "TB",
        "Sg0", "Sg1", "T2A", "T2B", "T4A", "T4B", "T8A", "T8B", "Z2A", "Z2B", "UA", "UB",
        "StA", "StB", "bonus", "gate"]
PO_C = ["rt", "vs", "vgs", "kd", "bh", "kh", "stp", "rk"]
PE_P = ["ymean", "orms", "yvar"]
AC_P = ["osq", "ysq", "yln", "oln", "rstd"]
DV_P = ["yc", "yn", "on", "ybonus", "y"]
PO_P = ["yw", "yb", "o"]


def program(nc, x_prompt, x_sample, state_gla, state_rwkv, state_rwkv_shift, cache_ffn_conv,
            norm_mix, w_in, gla_gate_w2, gla_gate_b, gla_norm_w, rwkv_mu, rwkv_w0, rwkv_w2,
            rwkv_a0, rwkv_a2, rwkv_g2, rwkv_k_k, rwkv_k_a, rwkv_r_k, rwkv_ln_w, rwkv_ln_b,
            w_out, norm_ffn, ffn_w_up, ffn_conv_w, ffn_conv_b, ffn_w_down, norm_final,
            y_prompt, y_sample, gla_p, rwkv_p, shift_p, conv_p, gla_s, rwkv_s, shift_s, conv_s):
    with ExitStack() as ctx:
        def sb(name, shape, dt=F32, scope=ctx):
            return scope.enter_context(nc.sbuf_tensor(name, shape, dt))

        def sem(name):
            return ctx.enter_context(nc.semaphore(name))

        x = sb("x", [P, KT, TOK])
        ident = sb("ident", [P, P])
        ident2 = sb("ident2", [P, C])
        mean128 = sb("mean128", [P, P])
        mean64 = sb("mean64", [P, P])
        m_di = sb("m_di", [P, P])
        m_si = sb("m_si", [P, P])
        m_d = sb("m_d", [P, C])
        m_e = sb("m_e", [P, C])
        restart = sb("restart", [P, NCH * CP], BF16)
        rows_a = sb("rows_a", [NA, P])
        rows_b = sb("rows_b", [NB, P])
        par = sb("par", [P, NA + NB])
        scal = sb("scal", [P, 3])
        rowout = sb("rowout", [P, 2, P])
        one_ka = sb("one_ka", [P, NP])
        w2a2 = sb("w2a2", [P, RC])
        g2 = sb("g2", [P, RC])
        gw2 = sb("gw2", [P, GK])
        bonus_w = sb("bonus_w", [P, NP, P])
        last_rows = sb("last_rows", [P, 2, RT])
        last_conv = sb("last_conv", [P, 4, F // P])
        raw = [sb(f"raw{s}", [P, FT * P]) for s in range(2)]
        whi = [sb(f"whi{s}", [P, FT * P], F32R) for s in range(2)]
        wlo = [sb(f"wlo{s}", [P, FT * P], F32R) for s in range(2)]
        T = [sb(f"T{i}", [P, 580]) for i in range(4)]
        with ExitStack() as s1:
            xh = sb("xh", [P, KT, TOK], F32R, s1)
            xl = sb("xl", [P, KT, TOK], F32R, s1)
        work = sb("work", [P, 2 * KT * TOK])
        taken = 0

        def cut(shape):
            nonlocal taken
            sizes, n = shape[1:], 1
            for size in sizes:
                n *= size
            piece = work[:, taken:taken + n]
            taken += n
            assert taken <= 2 * KT * TOK
            names = "abcd"[:len(sizes)]
            return piece.rearrange(f"p ({' '.join(names)}) -> p {' '.join(names)}",
                                   **dict(zip(names[1:], sizes[1:])))

        Pp = cut([P, NP, CP])
        Pinv = cut([P, NP, C])
        AR = cut([P, NP, 2 * C])
        Bt = cut([P, NP, C])
        Kt = cut([P, NP, C])
        Bh = cut([P, NP, C])
        Kh = cut([P, NP, C])
        Vs = cut([P, NP, C])
        StP = cut([P, NP, C])
        rk = cut([P, NP, C])
        QM = cut([P, NP, 2 * C])
        KM = cut([P, NP, 2 * C])
        Dm = cut([P, NP, C])
        Em = cut([P, NP, C])
        Ta = cut([P, NP, C])
        Tb = cut([P, NP, C])
        sq2 = cut([P, 2, 2, 2, C])
        sq4 = cut([P, 2, 2, 2, C])
        tok = cut([P, 2, 3, 2, C])
        St = cut([P, NP, C])
        Ych = cut([P, NP, C])
        Sg = cut([P, 2, GDV])
        Eg = cut([P, 2, C])
        Ei = cut([P, 2, C])
        qe = cut([P, 2, C])
        ke = cut([P, 2, C])
        kd = cut([P, 2, C])
        Vgs = cut([P, GH, C])
        scm = cut([P, 2, C])
        gtok = cut([P, 2 * GDV + 2 * C])
        Och = cut([P, GH, C])
        Yc = T[0][:, 0:NP * C].rearrange("p (a b) -> p a b", b=C)
        On = T[0][:, NP * C:2 * NP * C].rearrange("p (a b) -> p a b", b=C)
        SQ = T[1][:, 0:2 * NP * C]
        SQy = T[1][:, 0:NP * C].rearrange("p (a b) -> p a b", b=C)
        SQo = T[1][:, NP * C:2 * NP * C].rearrange("p (a b) -> p a b", b=C)
        BV = T[2][:, 0:NP * C].rearrange("p (a b) -> p a b", b=C)
        Gt = T[2][:, NP * C:2 * NP * C].rearrange("p (a b) -> p a b", b=C)
        Sraw = T[3][:, 0:NP * C].rearrange("p (a b) -> p a b", b=C)
        with ExitStack() as s2:
            hh = sb("hh", [P, FT, TOK], F32R, s2)
            hl = sb("hl", [P, FT, TOK], F32R, s2)
            up = sb("up", [P, 4 + TOK], scope=s2)
            cv = sb("cv", [P, 2 + TOK], scope=s2)
            gl = sb("gl", [P, 2 + TOK], scope=s2)
            hf = sb("hf", [P, TOK], scope=s2)
        with ExitStack() as s2:
            xin = sb("xin", [P, 5, D], scope=s2)
            yout = sb("yout", [P, 2, D], scope=s2)
            nsq = [sb(f"nsq{i}", [P, TOK], scope=s2) for i in range(2)]
            nln = sb("nln", [P, TOK], scope=s2)
            nrs = sb("nrs", [P, TOK], scope=s2)
            nt = [sb(f"nt{i}", [P, TOK], scope=s2) for i in range(2)]
        R = sb("R", [P, RT, TOK])
        KK = sb("KK", [P, NP, TOK])
        KA = sb("KA", [P, NP, TOK])
        cum = sb("cum", [P, NP, NCH * CP])
        G = sb("G", [P, GT, TOK])
        cg = sb("cg", [P, 2, NCH * CP])
        SgO = R[:, 12, 0:2 * GDV].rearrange("p (a b) -> p a b", b=GDV)
        StT = R[:, 12, 2 * GDV:2 * GDV + NP * C].rearrange("p (a b) -> p a b", b=C)

        PS = [ctx.enter_context(nc.psum_tensor(f"ps{i}", [P, 1024], F32)) for i in range(4)]

        def bank(b):
            return PS[b // 2][:, 512 * (b % 2):512 * (b % 2) + 512]

        pq = [bank(0), bank(2)]
        tt = [bank(1), bank(3)]
        gm, oE, oO, stat = bank(4), bank(5), bank(6), bank(7)
        nsum = PS[2]

        def pair3(ap, n=C):
            return ap.rearrange("p (a b) -> p a b", b=n)

        def pcol(name, j=0, n=1):
            at, _ = ROWS_A[name] if name in ROWS_A else (NA + ROWS_B[name][0], 0)
            return par[:, at + j:at + j + n]

        x_loaded = sem("x_loaded")
        rows_loaded = sem("rows_loaded")
        small_loaded = sem("small_loaded")
        states_loaded = sem("states_loaded")
        w_loaded = [sem(f"w_loaded{s}") for s in range(2)]
        w_hi = [sem(f"w_hi{s}") for s in range(2)]
        w_lo = [sem(f"w_lo{s}") for s in range(2)]
        tile_done = [sem(f"tile_done{s}") for s in range(2)]
        psum_free = [sem(f"psum_free{s}") for s in range(2)]
        consts = sem("consts")
        x_turned = sem("x_turned")
        x_copied = sem("x_copied")
        par_turned = sem("par_turned")
        par_ready = sem("par_ready")
        n_sq = sem("n_sq")
        n_sum = sem("n_sum")
        n_rs = sem("n_rs")
        n_t = sem("n_t")
        n_hi = sem("n_hi")
        n_lo = sem("n_lo")
        r_prev = sem("r_prev")
        r_dve = sem("r_dve")
        pre_pe = sem("pre_pe")
        pre_act = sem("pre_act")
        pre_dve = sem("pre_dve")
        st_pe = sem("st_pe")
        st_dve = sem("st_dve")
        pe_c, ac_c, dv_c, po_c = sem("pe_c"), sem("ac_c"), sem("dv_c"), sem("po_c")
        pe_p, ac_p, dv_p, po_p = sem("pe_p"), sem("ac_p"), sem("dv_p"), sem("po_p")
        m_hi = sem("m_hi")
        m_lo = sem("m_lo")
        up_pad = sem("up_pad")
        f_dve, f_gelu, f_hi = sem("f_dve"), sem("f_gelu"), sem("f_hi")
        kept = sem("kept")
        waited = sem("waited")
        states_out = sem("states_out")
        rows_turned, rows_copied = sem("rows_turned"), sem("rows_copied")
        y_turned, y_copied = sem("y_turned"), sem("y_copied")
        stored = sem("stored")
        y_stored = [sem(f"y_stored{i}") for i in range(2)]

        def apart(engine):
            engine.sem_inc(waited)

        block = ctx.enter_context(nc.Block())
        NORMS = 2
        BLOCKS = [(0, DEC)] + [(DEC + P * b, P) for b in range(SEQ // P)]

        @block.sync
        def _(sp):
            sp.dma_start(xin[0:DEC, 0, :], x_sample[0]).then_inc(x_loaded, 16)
            sp.dma_start(xin[:, 1:5, :], x_prompt[0].rearrange("(b p) d -> p b d", p=P)).then_inc(x_loaded, 16)
            with sp.Fori(0, DEPTH) as l:
                def rows(name, src):
                    t, o, n = (rows_a, *ROWS_A[name]) if name in ROWS_A else (rows_b, *ROWS_B[name])
                    sp.dma_start(t[o:o + n, :], src).then_inc(rows_loaded, 16)

                sp.wait_ge(par_turned, l)
                rows("norm_mix", norm_mix[l].rearrange("(k p) -> k p", p=P))
                rows("norm_ffn", norm_ffn[l].rearrange("(k p) -> k p", p=P))
                rows("norm_final", norm_final.rearrange("(k p) -> k p", p=P))
                rows("gate_b", gla_gate_b[l].rearrange("(k p) -> k p", p=P))
                rows("gla_w", gla_norm_w[l].rearrange("(k p) -> k p", p=P))
                rows("mu", rwkv_mu[l].rearrange("(k p) -> k p", p=P))
                for name, src in (("w0", rwkv_w0), ("a0", rwkv_a0), ("k_k", rwkv_k_k), ("k_a", rwkv_k_a),
                                  ("ln_w", rwkv_ln_w), ("ln_b", rwkv_ln_b)):
                    rows(name, src[l].rearrange("(k p) -> k p", p=P))
                rows("r_k", rwkv_r_k[l].rearrange("(k h) n -> k (h n)", h=2))
                rows("shift", state_rwkv_shift[l, 0].rearrange("(k p) -> k p", p=P))
                rows("cache", cache_ffn_conv[l, 0].rearrange("r (k p) -> (r k) p", p=P))
                rows("conv_w", ffn_conv_w[l].rearrange("r (k p) -> (r k) p", p=P))
                rows("conv_b", ffn_conv_b[l].rearrange("(k p) -> k p", p=P))

                def load(s, k, dst, src):
                    sp.wait_ge(w_lo[s], k)
                    sp.dma_start(dst, src).then_inc(w_loaded[s], 16)

                def in_tile(s, k, col):
                    load(s, k, raw[s][:, 0:KT * P].rearrange("p (k m) -> p k m", m=P),
                         w_in[l].rearrange("(k p) c -> p k c", p=P)[:, :, bass.ds(col, P)])

                with sp.Fori(0, RT // 2) as it:
                    for s in range(2):
                        in_tile(s, turn(s, l, PAIRS["rwkv"] + it, False), GLA_COLS + (2 * it + s) * P)
                sp.wait_ge(consts, N_CONSTS)
                sp.dma_start(w2a2[0:64, :], rwkv_w2[l]).then_inc(small_loaded, 16)
                sp.dma_start(w2a2[64:128, :], rwkv_a2[l]).then_inc(small_loaded, 16)
                sp.dma_start(g2[:, :], rwkv_g2[l]).then_inc(small_loaded, 16)
                sp.dma_start(gw2[LR_AT:LR_AT + 16, :], gla_gate_w2[l]).then_inc(small_loaded, 16)
                in_tile(0, turn(0, l, PAIRS["gla"], False), GLA_COLS - 16 - LR_AT)
                with sp.Fori(0, GT // 2) as it:
                    for s in range(2):
                        in_tile(s, turn(s, l, PAIRS["gla"] + it), (2 * it + s) * P)
                sp.wait_ge(tile_done[0], turn(0, l, PAIRS["out"]))
                sp.wait_ge(tile_done[1], turn(1, l, PAIRS["out"]))
                sp.wait_ge(pre_dve, (l + 1) * N_PRE_DVE)
                for hp in range(2):
                    h = slice(64 * hp, 64 * hp + 64)
                    sp.dma_start(Sg[h, :, :], state_gla[l, 0].rearrange("(q h) d v -> h d q v", h=2)[hp])\
                      .then_inc(states_loaded, 16)
                    sp.dma_start(Sraw[h, :, :], state_rwkv[l, 0].rearrange("(q h) v k -> h v q k", h=2)[hp])\
                      .then_inc(states_loaded, 16)
                with sp.Fori(0, KT // 2) as it:
                    for s in range(2):
                        load(s, turn(s, l, PAIRS["out"] + it), raw[s][:, 0:KT * P].rearrange("p (k m) -> p k m", m=P),
                             w_out[l].rearrange("(k p) c -> p k c", p=P)[:, :, bass.ds((2 * it + s) * P, P)])
                with sp.Fori(0, HALVES) as h:
                    with sp.Fori(0, FT) as it:
                        for s in range(2):
                            load(s, turn(s, l, PAIRS["ffn"] + h * FFN_PAIRS + it),
                                 raw[s][:, 0:KT * P].rearrange("p (k m) -> p k m", m=P),
                                 ffn_w_up[l].rearrange("(k p) c -> p k c", p=P)[:, :, bass.ds(s * F + (h * FT + it) * P, P)])
                    with sp.Fori(0, KT // 2) as it:
                        for s in range(2):
                            load(s, turn(s, l, PAIRS["ffn"] + h * FFN_PAIRS + FT + it),
                                 raw[s][:, :].rearrange("p (k m) -> p k m", m=P),
                                 ffn_w_down[l].rearrange("(g k p) c -> g p k c", p=P, g=HALVES)[h][:, :, bass.ds((2 * it + s) * P, P)])

        @block.gpsimd
        def _(po):
            e = nc.gpsimd
            n = 0

            def const(ins):
                nonlocal n
                n += 1
                ins.then_inc(consts, 1)
                po.wait_ge(consts, n)

            def keep(out, pattern, base, mult):
                const(e.affine_select(out=out, in_=out, compare_op=ALU.is_ge, fill=0.0, base=base,
                                      pattern=pattern, channel_multiplier=mult))

            const(e.memset(ident[:, :], 1.0))
            keep(ident[:, :], [[1, P]], 0, -1)
            keep(ident[:, :], [[-1, P]], 0, 1)
            for j, value in enumerate((EPS, 10 * LN2, GN_EPS)):
                const(e.memset(scal[:, j:j + 1], value))
            const(e.memset(mean128[:, :], 1.0 / 128))
            const(e.memset(mean64[:, :], 0.0))
            for m in (ident2, m_di, m_si, m_d, m_e):
                const(e.memset(m[:, :], 1.0))
            const(e.memset(restart[:, :], 1.0))
            const(e.memset(restart[:, :].rearrange("p (c t) -> p c t", t=CP)[:, :, 0:1], 0.0))
            const(e.memset(gw2[:, :], 0.0))
            for hp in range(2):
                h = slice(64 * hp, 64 * hp + 64)
                const(e.memset(mean64[h, 64 * hp:64 * hp + 64], 1.0 / 64))
                keep(ident2[h, :], [[1, C]], 0, -1)
                keep(ident2[h, :], [[-1, C]], 0, 1)
                keep(m_di[h, C:2 * C], [[1, C]], 0, -1)
                keep(m_si[h, C:2 * C], [[1, C]], 0, -1)
                keep(m_si[h, 0:C], [[1, C]], -1, -1)
                keep(m_di[h, 0:C], [[1, C]], -1, -1)
                keep(m_d[h, :], [[-1, C]], -1, 1)
                keep(m_e[h, :], [[-1, C]], -1, 1)
                for m in (m_di[h, 0:C], m_d[h, :]):
                    v = m.rearrange("p (b j) -> p b j", j=16)
                    keep(v, [[-16, 4], [0, 16]], 0, 1)
                    keep(v, [[16, 4], [0, 16]], 15, -1)
                keep(m_e[h, :].rearrange("p (b j) -> p b j", j=16), [[-16, 4], [0, 16]], -16, 1)

            def split(s, k, width):
                po.wait_ge(w_loaded[s], 16 * k + 16)
                po.wait_ge(tile_done[s], k)
                apart(po)
                e.tensor_copy(whi[s][:, 0:width], raw[s][:, 0:width]).then_inc(w_hi[s], 1)
                po.wait_ge(w_hi[s], k + 1)
                e.tensor_tensor(wlo[s][:, 0:width], raw[s][:, 0:width], whi[s][:, 0:width].bitcast(F32),
                                ALU.subtract).then_inc(w_lo[s], 1)

            assert n == N_CONSTS, n
            with po.Fori(0, DEPTH) as l:
                with po.Fori(0, RT // 2) as it:
                    for s in range(2):
                        split(s, turn(s, l, PAIRS["rwkv"] + it, False), KT * P)
                split(0, turn(0, l, PAIRS["gla"], False), KT * P)
                with po.Fori(0, GT // 2) as it:
                    for s in range(2):
                        split(s, turn(s, l, PAIRS["gla"] + it), KT * P)
                for s in range(2):
                    split(s, turn(s, l, PAIRS["out"]), KT * P)

                def after(i, cc):
                    m = l * NCH + i
                    po.wait_ge(dv_p, m * len(DV_P) + DV_P.index("yn") + 1)
                    e.tensor_tensor(Yc, Yc, pcol("ln_w", 0, NP).unsqueeze(2).broadcast_to([P, NP, C]), ALU.mult)\
                     .then_inc(po_p, 1)
                    po.wait_ge(po_p, m * len(PO_P) + 1)
                    e.tensor_tensor(Yc, Yc, pcol("ln_b", 0, NP).unsqueeze(2).broadcast_to([P, NP, C]), ALU.add)\
                     .then_inc(po_p, 1)
                    po.wait_ge(dv_p, m * len(DV_P) + DV_P.index("on") + 1)
                    e.tensor_tensor(G[:, 4:8, cc], On, G[:, 8:12, cc], ALU.mult).then_inc(po_p, 1)

                def chunk(i, first):
                    n = l * NCH + i
                    cc = bass.ds(i * C, C)

                    def mine(name):
                        po.wait_ge(po_c, n * len(PO_C) + PO_C.index(name) + 1)

                    def act(name):
                        po.wait_ge(ac_c, n * len(AC_C) + AC_C.index(name) + 1)

                    def dve(name):
                        po.wait_ge(dv_c, n * len(DV_C) + DV_C.index(name) + 1)

                    if not first:
                        po.wait_ge(pe_c, (n - 1) * len(PE_C) + PE_C.index("YB") + 1)
                    else:
                        po.wait_ge(st_dve, (l * 3) + 1)
                        for s in range(2):
                            po.wait_ge(psum_free[s], turn(s, l, PAIRS["out"]))
                    act("P")
                    e.tensor_tensor(AR[:, :, C:2 * C], R[:, 0:4, cc], Pp[:, :, 1:CP], ALU.mult).then_inc(po_c, 1)
                    e.tensor_copy(Vs[:, :, :], R[:, 8:12, cc]).then_inc(po_c, 1)
                    e.tensor_copy(Vgs[:, :, :], G[:, 4:8, cc]).then_inc(po_c, 1)
                    dve("ke")
                    act("Eg")
                    e.tensor_tensor(kd[:, :, :], ke[:, :, :], Eg[:, :, C - 1:C].broadcast_to([P, 2, C]), ALU.mult)\
                     .then_inc(po_c, 1)
                    last = Pp[:, :, C:CP].broadcast_to([P, NP, C])
                    dve("bt")
                    e.tensor_tensor(Bh[:, :, :], Bt[:, :, :], last, ALU.mult).then_inc(po_c, 1)
                    dve("kt")
                    e.tensor_tensor(Kh[:, :, :], Kt[:, :, :], last, ALU.mult).then_inc(po_c, 1)
                    if not first:
                        po.wait_ge(dv_c, (n - 1) * len(DV_C) + DV_C.index("StB") + 1)
                        po.wait_ge(st_dve, l * 3 + 3)
                    e.tensor_tensor(StP[:, :, :], St[:, :, :], last, ALU.mult).then_inc(po_c, 1)
                    if not first:
                        po.wait_ge(pe_c, (n - 1) * len(PE_C) + PE_C.index("bonus") + 1)
                    e.tensor_tensor(rk[:, :, :], R[:, 0:4, cc], R[:, 4:8, cc], ALU.mult).then_inc(po_c, 1)

                chunk(0, True)
                with po.Fori(1, NCH) as i:
                    chunk(i, False)
                    after(i - 1, bass.ds((i - 1) * C, C))
                after(NCH - 1, bass.ds((NCH - 1) * C, C))
                with po.Fori(1, KT // 2) as it:
                    for s in range(2):
                        split(s, turn(s, l, PAIRS["out"] + it), KT * P)
                with po.Fori(0, HALVES) as h:
                    with po.Fori(0, FT) as it:
                        for s in range(2):
                            split(s, turn(s, l, PAIRS["ffn"] + h * FFN_PAIRS + it), KT * P)
                    with po.Fori(0, KT // 2) as it:
                        for s in range(2):
                            split(s, turn(s, l, PAIRS["ffn"] + h * FFN_PAIRS + FT + it), FT * P)

        @block.tensor
        def _(pe):
            e = nc.tensor

            def both(out, lhsT, rhs, start, stop):
                e.matmul(out[:, 0:512], lhsT, rhs[:, 0:512], start=start, stop=stop)
                return e.matmul(out[:, 512:TOK], lhsT, rhs[:, 512:TOK], start=start, stop=stop)

            def dense(s, k, hi, lo, kts, first_rhs=None):
                pe.wait_ge(w_lo[s], k + 1)
                pe.wait_ge(psum_free[s], k)
                for kt in range(kts):
                    if first_rhs is not None:
                        first_rhs(kt)
                    wh = whi[s][:, kt * P:(kt + 1) * P]
                    wl = wlo[s][:, kt * P:(kt + 1) * P]
                    for lhsT, rhs, a, z in ((wh, hi[:, kt], kt == 0, False), (wh, lo[:, kt], False, False),
                                            (wl, hi[:, kt], False, kt == kts - 1)):
                        mm = both(PS[s], lhsT, rhs, a, z)
                mm.then_inc(tile_done[s], 1)

            pe.wait_ge(consts, N_CONSTS)
            for b, (t0, w) in enumerate(BLOCKS):
                pe.wait_ge(x_loaded, 32)
                if b >= 2:
                    pe.wait_ge(x_copied, b - 1)
                for k in range(KT):
                    mm = e.transpose(PS[b % 2][:, k * P:k * P + w], xin[0:w, b, k * P:(k + 1) * P], ident[0:w, 0:w])
                mm.then_inc(x_turned, 1)

            def norm_sum(c):
                for k in range(KT):
                    pe.wait_ge(n_sq, c * KT + k + 1)
                    e.matmul(nsum[:, 0:512], mean128[:, :], nsq[k % 2][:, 0:512], start=k == 0, stop=k == KT - 1)
                    e.matmul(nsum[:, 512:TOK], mean128[:, :], nsq[k % 2][:, 512:TOK],
                             start=k == 0, stop=k == KT - 1).then_inc(n_sum, 1)

            with pe.Fori(0, DEPTH) as l:
                pe.wait_ge(rows_loaded, (l + 1) * 16 * N_ROWS)
                pe.wait_ge(x_copied, len(BLOCKS))
                e.transpose(PS[3][:, 0:NA], rows_a[:, :], ident[0:NA, 0:NA])
                e.transpose(PS[3][:, NA:NA + NB], rows_b[:, :], ident[0:NB, 0:NB]).then_inc(par_turned, 1)
                norm_sum(l * NORMS)

                def hi_lo(c):
                    def need(kt):
                        pe.wait_ge(n_lo, c * KT + kt + 1)
                    return need

                for s in range(2):
                    dense(s, turn(s, l, PAIRS["rwkv"], False), xh, xl, KT, hi_lo(l * NORMS) if s == 0 else None)
                with pe.Fori(1, RT // 2) as it:
                    for s in range(2):
                        dense(s, turn(s, l, PAIRS["rwkv"] + it, False), xh, xl, KT)

                pe.wait_ge(small_loaded, (l + 1) * 64)
                for s in range(2):
                    pe.wait_ge(psum_free[s], turn(s, l, PAIRS["gla"], False))
                pe.wait_ge(pre_act, l * N_PRE_ACT + A_TANH)
                pe.wait_ge(par_ready, l * 3 + 3)
                for p in range(NP):
                    w = w2a2[0:64, p * P:(p + 1) * P]
                    v = R[0:64, 12]
                    e.matmul(PS[p][:, 0:512], w, v[:, 0:512], start=True, stop=True)
                    e.matmul(PS[p][:, 512:TOK], w, v[:, 512:TOK], start=True, stop=True).then_inc(pre_pe, 1)
                for p in range(NP):
                    pe.wait_ge(pre_act, l * N_PRE_ACT + A_W + p)
                    w = w2a2[64:128, p * P:(p + 1) * P]
                    v = R[64:128, 12]
                    e.matmul(PS[p][:, 0:512], w, v[:, 0:512], start=True, stop=True)
                    e.matmul(PS[p][:, 512:TOK], w, v[:, 512:TOK], start=True, stop=True).then_inc(pre_pe, 1)
                for p in range(NP):
                    pe.wait_ge(pre_act, l * N_PRE_ACT + A_A + p)
                    pe.wait_ge(pre_act, l * N_PRE_ACT + A_SQ + p)
                    both(PS[p], mean64[:, :], T[p], True, True).then_inc(pre_pe, 1)

                pe.wait_ge(pre_dve, l * N_PRE_DVE + D_MAX + 1)
                dense(0, turn(0, l, PAIRS["gla"], False), xh, xl, KT)
                pe.wait_ge(psum_free[0], turn(0, l, PAIRS["gla"], False) + 1)
                pe.wait_ge(pre_dve, l * N_PRE_DVE + D_MAX + 3)
                for q in range(2):
                    w = gw2[LR_AT:P, q * P:(q + 1) * P]
                    v = R[LR_AT:P, 12]
                    e.matmul(PS[2 + q][:, 0:512], w, v[:, 0:512], start=True, stop=True)
                    e.matmul(PS[2 + q][:, 512:TOK], w, v[:, 512:TOK], start=True, stop=True).then_inc(pre_pe, 1)
                with pe.Fori(0, GT // 2) as it:
                    for s in range(2):
                        dense(s, turn(s, l, PAIRS["gla"] + it), xh, xl, KT)

                def turn_state(src):
                    for p in range(NP):
                        for hp in range(2):
                            h = slice(64 * hp, 64 * hp + 64)
                            mm = e.matmul(stat[h, p * C:(p + 1) * C], src[h, p, :], ident2[h, :], start=True, stop=True)
                    mm.then_inc(st_pe, 1)

                pe.wait_ge(states_loaded, (l + 1) * 64)
                for s in range(2):
                    pe.wait_ge(psum_free[s], turn(s, l, PAIRS["out"]))
                pe.wait_ge(pre_dve, (l + 1) * N_PRE_DVE)
                apart(pe)
                turn_state(Sraw)
                pe.wait_ge(st_dve, l * 3 + 1)

                def after_a(i):
                    m = l * NCH + i
                    pe.wait_ge(ac_c, m * len(AC_C) + AC_C.index("YB") + 1)
                    pe.wait_ge(dv_c, m * len(DV_C) + DV_C.index("gate") + 1)
                    e.matmul(stat[:, 0:NP * C], mean64[:, :], Ych[:, :, :].rearrange("p a b -> p (a b)"),
                             start=True, stop=True).then_inc(pe_p, 1)
                    pe.wait_ge(ac_p, m * len(AC_P) + AC_P.index("osq") + 1)
                    e.matmul(oE[:, NP * C:2 * NP * C], mean128[:, :], SQ[:, NP * C:2 * NP * C],
                             start=True, stop=True).then_inc(pe_p, 1)

                def after_b(i):
                    m = l * NCH + i
                    pe.wait_ge(ac_p, m * len(AC_P) + AC_P.index("ysq") + 1)
                    e.matmul(oE[:, 0:NP * C], mean64[:, :], SQ[:, 0:NP * C], start=True, stop=True)\
                     .then_inc(pe_p, 1)

                def chunk(i, first):
                    n = l * NCH + i

                    def act(name, m=n):
                        pe.wait_ge(ac_c, m * len(AC_C) + AC_C.index(name) + 1)
                        apart(pe)

                    def dve(name, m=n):
                        pe.wait_ge(dv_c, m * len(DV_C) + DV_C.index(name) + 1)
                        apart(pe)

                    def pool(name, m=n):
                        pe.wait_ge(po_c, m * len(PO_C) + PO_C.index(name) + 1)
                        apart(pe)

                    def heads(X):
                        for q in range(2):
                            for hp in range(2):
                                yield 2 * X + q, slice(64 * hp, 64 * hp + 64), q

                    if not first:
                        after_a(i - 1)
                    dve("ke")
                    for q in range(2):
                        for hp in range(2):
                            h = slice(64 * hp, 64 * hp + 64)
                            mm = e.matmul(gm[h, q * C:(q + 1) * C], ke[h, q, :], qe[h, q, :], start=True, stop=True)
                    mm.then_inc(pe_c, 1)
                    pool("kd")
                    for q in range(2):
                        for hp in range(2):
                            h = slice(64 * hp, 64 * hp + 64)
                            e.matmul(oO[h, q * GDV:(q + 1) * GDV], Vgs[:, 2 * q + hp, :], ident[:, :],
                                     start=True, stop=True)
                            mm = e.matmul(oO[h, 2 * GDV + q * C:2 * GDV + (q + 1) * C], kd[h, q, :], ident2[h, :],
                                          start=True, stop=True)
                    mm.then_inc(pe_c, 1)
                    if not first:
                        after_b(i - 1)
                    dve("kt")
                    pool("rt")
                    for X in range(2):
                        for p, h, q in heads(X):
                            e.matmul(pq[X][h, q * P:(q + 1) * P], Bt[h, p, :], AR[h, p, :], start=True, stop=True)
                            e.matmul(pq[X][h, 256 + q * P:256 + (q + 1) * P], Kt[h, p, :], AR[h, p, :],
                                     start=True, stop=True)
                            mm = e.matmul(tt[X][h, q * C:(q + 1) * C], AR[h, p, 0:C], Bt[h, p, :],
                                          start=True, stop=True)
                        mm.then_inc(pe_c, 1)
                    dve("g_scores")
                    act("g_tok")
                    if not first:
                        pe.wait_ge(ac_p, (n - 1) * len(AC_P) + AC_P.index("oln") + 1)
                    for q in range(2):
                        for hp, o in ((0, oE), (1, oO)):
                            h = slice(64 * hp, 64 * hp + 64)
                            e.matmul(o[:, q * C:(q + 1) * C], gtok[h, q * GDV:(q + 1) * GDV], scm[h, q, :],
                                     start=True, stop=False)
                            mm = e.matmul(o[:, q * C:(q + 1) * C], Sg[h, q, :], qe[h, q, :], start=False, stop=True)
                    mm.then_inc(pe_c, 1)
                    for q in range(2):
                        for hp in range(2):
                            h = slice(64 * hp, 64 * hp + 64)
                            mm = e.matmul(gm[h, q * GDV:(q + 1) * GDV],
                                          gtok[h, 2 * GDV + q * C:2 * GDV + (q + 1) * C],
                                          gtok[h, q * GDV:(q + 1) * GDV], start=True, stop=True)
                    mm.then_inc(pe_c, 1)
                    pool("kh")
                    for X, N in ((0, "A"), (1, "B")):
                        dve("K" + N)
                        for a, src in enumerate((Bh, Kh, Vs)):
                            for p, h, q in heads(X):
                                mm = e.matmul(pq[X][h, (2 * a + q) * C:(2 * a + q + 1) * C], src[h, p, :],
                                              ident2[h, :], start=True, stop=True)
                        mm.then_inc(pe_c, 1)
                    for X, N in ((0, "A"), (1, "B")):
                        dve("E" + N)
                        for p, h, q in heads(X):
                            e.matmul(tt[X][h, q * C:(q + 1) * C], QM[h, p, 0:C], Dm[h, p, :], start=True, stop=True)
                            mm = e.matmul(tt[X][h, (2 + q) * C:(3 + q) * C], Dm[h, p, :], QM[h, p, 0:C],
                                          start=True, stop=True)
                        mm.then_inc(pe_c, 1)
                    for X, N in ((0, "A"), (1, "B")):
                        act("tok" + N)
                        act("sq2" + N)
                        for p, h, q in heads(X):
                            e.matmul(pq[X][h, q * C:(q + 1) * C], sq2[h, X, 1, q, :], sq2[h, X, 0, q, :],
                                     start=True, stop=True)
                            mm = e.matmul(pq[X][h, (2 + q) * C:(3 + q) * C], sq2[h, X, 0, q, :], sq2[h, X, 1, q, :],
                                          start=True, stop=True)
                        mm.then_inc(pe_c, 1)
                        dve("T" + N)
                        for p, h, q in heads(X):
                            mm = e.matmul(tt[X][h, q * C:(q + 1) * C], sq2[h, X, 0, q, :], Ta[h, p, :],
                                          start=True, stop=True)
                        mm.then_inc(pe_c, 1)
                    for X, N in ((0, "A"), (1, "B")):
                        act("sq4" + N)
                        for p, h, q in heads(X):
                            mm = e.matmul(pq[X][h, q * C:(q + 1) * C], sq4[h, X, 1, q, :], sq4[h, X, 0, q, :],
                                          start=True, stop=True)
                        mm.then_inc(pe_c, 1)
                        dve("T2" + N)
                        for p, h, q in heads(X):
                            mm = e.matmul(tt[X][h, q * C:(q + 1) * C], sq4[h, X, 0, q, :], Tb[h, p, :],
                                          start=True, stop=True)
                        mm.then_inc(pe_c, 1)
                    for X, N in ((0, "A"), (1, "B")):
                        act("sq8" + N)
                        dve("T4" + N)
                        for p, h, q in heads(X):
                            mm = e.matmul(tt[X][h, q * C:(q + 1) * C], sq2[h, X, 0, q, :], Ta[h, p, :],
                                          start=True, stop=True)
                        mm.then_inc(pe_c, 1)
                    for X, N in ((0, "A"), (1, "B")):
                        dve("T8" + N)
                        for p, h, q in heads(X):
                            e.matmul(pq[X][h, q * C:(q + 1) * C], Tb[h, p, :], Em[h, p, :], start=True, stop=True)
                            mm = e.matmul(pq[X][h, (2 + q) * C:(3 + q) * C], Em[h, p, :], Tb[h, p, :],
                                          start=True, stop=True)
                        mm.then_inc(pe_c, 1)
                    for X, N in ((0, "A"), (1, "B")):
                        act("F" + N)
                        for p, h, q in heads(X):
                            mm = e.matmul(tt[X][h, q * C:(q + 1) * C], sq4[h, X, 0, q, :], sq4[h, X, 1, q, :],
                                          start=True, stop=True)
                        mm.then_inc(pe_c, 1)
                    if not first:
                        dve("StB", n - 1)
                        pe.wait_ge(st_dve, l * 3 + 3)
                        apart(pe)
                    for X, N in ((0, "A"), (1, "B")):
                        for p, h, q in heads(X):
                            e.matmul(pq[X][h, q * C:(q + 1) * C], AR[h, p, 0:C], St[h, p, :], start=True, stop=False)
                            mm = e.matmul(pq[X][h, q * C:(q + 1) * C], KM[h, p, 0:C], tok[h, X, 2, q, :],
                                          start=False, stop=True)
                        mm.then_inc(pe_c, 1)
                    for X, N in ((0, "A"), (1, "B")):
                        act("F2" + N)
                        act("Z" + N)
                        for p, h, q in heads(X):
                            mm = e.matmul(tt[X][h, q * C:(q + 1) * C], Tb[h, p, :], Em[h, p, :], start=True, stop=True)
                        mm.then_inc(pe_c, 1)
                    for X, N in ((0, "A"), (1, "B")):
                        act("Z1" + N)
                        for p, h, q in heads(X):
                            mm = e.matmul(pq[X][h, q * C:(q + 1) * C], sq4[h, X, 1, q, :], sq2[h, X, 0, q, :],
                                          start=True, stop=True)
                        mm.then_inc(pe_c, 1)
                    for X, N in ((0, "A"), (1, "B")):
                        dve("Z2" + N)
                        for p, h, q in heads(X):
                            mm = e.matmul(tt[X][h, q * C:(q + 1) * C], Dm[h, p, :], sq2[h, X, 1, q, :],
                                          start=True, stop=True)
                        mm.then_inc(pe_c, 1)
                    for X, N in ((0, "A"), (1, "B")):
                        dve("U" + N)
                        for p, h, q in heads(X):
                            o = tt[X][h, q * C:(q + 1) * C]
                            e.matmul(o, St[h, p, :], AR[h, p, C:2 * C], start=True, stop=False)
                            e.matmul(o, Ta[h, p, :], QM[h, p, C:2 * C], start=False, stop=False)
                            mm = e.matmul(o, tok[h, X, 2, q, :], KM[h, p, C:2 * C], start=False, stop=True)
                        mm.then_inc(pe_c, 1)
                        for p, h, q in heads(X):
                            o = pq[X][h, q * C:(q + 1) * C]
                            e.matmul(o, tok[h, X, 0, q, :], Ta[h, p, :], start=True, stop=False)
                            mm = e.matmul(o, tok[h, X, 1, q, :], tok[h, X, 2, q, :], start=False, stop=True)
                        mm.then_inc(pe_c, 1)
                    pool("rk")
                    if not first:
                        pe.wait_ge(dv_p, (n - 1) * len(DV_P) + DV_P.index("yc") + 1)
                    for p in range(NP):
                        e.matmul(stat[:, p * C:(p + 1) * C], bonus_w[:, p, :], rk[:, p, :], start=True, stop=True)
                        mm = e.matmul(stat[:, (NP + p) * C:(NP + p + 1) * C], g2[:, p * P:(p + 1) * P],
                                      R[:, 13, bass.ds(i * C, C)], start=True, stop=True)
                    mm.then_inc(pe_c, 1)

                chunk(0, True)
                pe.wait_ge(dv_c, (l * NCH) * len(DV_C) + len(DV_C))
                apart(pe)
                turn_state(St)
                pe.wait_ge(kept, l * 4 + 2)
                apart(pe)
                with pe.Fori(1, NCH) as i:
                    chunk(i, False)
                after_a(NCH - 1)
                after_b(NCH - 1)
                pe.wait_ge(dv_p, (l * NCH + NCH - 1) * len(DV_P) + DV_P.index("yc") + 1)
                apart(pe)
                turn_state(St)

                for s in range(2):
                    def need(kt):
                        pe.wait_ge(m_lo, l * KT + kt + 1)
                    dense(s, turn(s, l, PAIRS["out"]), xh, xl, KT, need if s == 0 else None)
                with pe.Fori(1, KT // 2) as it:
                    for s in range(2):
                        dense(s, turn(s, l, PAIRS["out"] + it), xh, xl, KT)

                norm_sum(l * NORMS + 1)
                pe.wait_ge(n_lo, (l * NORMS + 2) * KT)
                apart(pe)
                with pe.Fori(0, HALVES) as h:
                    with pe.Fori(0, FT) as it:
                        for s in range(2):
                            dense(s, turn(s, l, PAIRS["ffn"] + h * FFN_PAIRS + it), xh, xl, KT)
                    pe.wait_ge(f_dve, ((l * HALVES + h) * FT + FT) * F_STEPS)
                    apart(pe)
                    with pe.Fori(0, KT // 2) as it:
                        for s in range(2):
                            dense(s, turn(s, l, PAIRS["ffn"] + h * FFN_PAIRS + FT + it), hh, hl, FT)

                e.transpose(PS[3][0:2 * RT, 0:P], last_rows[:, :, :].rearrange("p a b -> p (a b)"), ident[:, :])
                e.transpose(PS[3][0:4 * (F // P), P:2 * P], last_conv[:, :, :].rearrange("p a b -> p (a b)"), ident[:, :])\
                 .then_inc(rows_turned, 1)
                pe.wait_ge(rows_copied, 2 * l + 2)

            norm_sum(DEPTH * NORMS)
            pe.wait_ge(n_t, (DEPTH * NORMS + 1) * KT)
            for b, (t0, w) in enumerate(BLOCKS):
                if b >= 2:
                    pe.wait_ge(y_copied, b - 1)
                for k in range(KT):
                    mm = e.transpose(PS[b % 2][0:w, k * P:(k + 1) * P], x[:, k, t0:t0 + w], ident[:, :])
                mm.then_inc(y_turned, 1)

        @block.scalar
        def _(ac):
            e = nc.scalar

            def norm(c):
                for k in range(KT):
                    if k >= 2:
                        ac.wait_ge(n_sum, c * KT + k - 1)
                    e.activation(nsq[k % 2][:, :], x[:, k, :], ACT.Square).then_inc(n_sq, 1)
                ac.wait_ge(n_sum, (c + 1) * KT)
                e.activation(nln[:, :], nsum[:, 0:TOK], ACT.Ln, scale=1.0 / KT, bias=scal[:, 0:1])\
                 .then_inc(n_rs, 1)
                ac.wait_ge(n_rs, 2 * c + 1)
                e.activation(nrs[:, :], nln[:, :], ACT.Exp, scale=-0.5).then_inc(n_rs, 1)

            def norm_hi(c):
                for k in range(KT):
                    ac.wait_ge(n_t, c * KT + k + 1)
                    e.activation(xh[:, k, :], nt[k % 2][:, :], ACT.Copy).then_inc(n_hi, 1)

            ac.wait_ge(x_copied, len(BLOCKS))
            ac.wait_ge(consts, N_CONSTS)
            with ac.Fori(0, DEPTH) as l:
                for s in range(2):
                    ac.wait_ge(psum_free[s], turn(s, l, 0, False))
                norm(l * NORMS)
                norm_hi(l * NORMS)
                with ac.Fori(0, RT // 2) as it:
                    for s in range(2):
                        ac.wait_ge(tile_done[s], turn(s, l, PAIRS["rwkv"] + it, False) + 1)
                        ac.wait_ge(psum_free[s], turn(s, l, PAIRS["rwkv"] + it, False))
                        e.activation(T[s][:, 1:1 + TOK], PS[s][:, 0:TOK], ACT.Copy).then_inc(r_prev, 1)
                for s in range(2):
                    ac.wait_ge(psum_free[s], turn(s, l, PAIRS["gla"], False))
                b = l * N_PRE_ACT
                e.activation(R[0:64, 12, :], R[0:64, 12, :], ACT.Tanh).then_inc(pre_act, 1)
                e.activation(R[:, 13, :], R[:, 13, :], ACT.Sigmoid).then_inc(pre_act, 1)
                ac.wait_ge(pre_dve, l * N_PRE_DVE + D_ZERO)
                for p in range(NP):
                    ac.wait_ge(pre_pe, l * N_PRE_PE + p + 1)
                    o = cum[:, p, :].rearrange("p (c t) -> p c t", t=CP)[:, :, 1:CP]
                    e.activation(o, PS[p][:, 0:TOK].rearrange("p (c t) -> p c t", t=C), ACT.Sigmoid,
                                 bias=pcol("w0", p)).then_inc(pre_act, 1)
                for p in range(NP):
                    ac.wait_ge(pre_pe, l * N_PRE_PE + NP + p + 1)
                    e.activation(KA[:, p, :], PS[p][:, 0:TOK], ACT.Sigmoid, bias=pcol("a0", p)).then_inc(pre_act, 1)
                for p in range(NP):
                    ac.wait_ge(pre_dve, l * N_PRE_DVE + D_KK + p)
                    e.activation(T[p][:, 0:TOK], KK[:, p, :], ACT.Square).then_inc(pre_act, 1)
                for p in range(NP):
                    ac.wait_ge(pre_dve, l * N_PRE_DVE + D_MAX + p)
                    e.activation(T[p][:, 0:TOK], T[p][:, 0:TOK], ACT.Ln, scale=float(2 ** 26)).then_inc(pre_act, 1)
                    ac.wait_ge(pre_act, b + A_LN + 2 * p)
                    e.activation(T[p][:, 0:TOK], T[p][:, 0:TOK], ACT.Exp, scale=-0.5, bias=scal[:, 1:2])\
                     .then_inc(pre_act, 1)
                ac.wait_ge(tile_done[0], turn(0, l, PAIRS["gla"], False) + 1)
                e.activation(R[LR_AT:P, 12, :], PS[0][LR_AT:P, 0:TOK], ACT.Copy).then_inc(psum_free[0], 1)
                for q in range(2):
                    ac.wait_ge(pre_dve, l * N_PRE_DVE + D_ABS + 2 * q)
                    e.activation(T[2 * q + 1][:, 0:TOK], T[2 * q + 1][:, 0:TOK], ACT.Exp, scale=-1.0).then_inc(pre_act, 1)
                    ac.wait_ge(pre_act, b + A_GE + 2 * q)
                    e.activation(T[2 * q + 1][:, 0:TOK], T[2 * q + 1][:, 0:TOK], ACT.Ln, bias=1.0).then_inc(pre_act, 1)
                with ac.Fori(0, 4) as it:
                    for s in range(2):
                        ac.wait_ge(tile_done[s], turn(s, l, PAIRS["gla"] + it) + 1)
                        e.activation(G[:, bass.ds(2 * it + s, 1), :], PS[s][:, 0:TOK].unsqueeze(1), ACT.Copy)\
                         .then_inc(psum_free[s], 1)
                with ac.Fori(4, 6) as it:
                    for s in range(2):
                        ac.wait_ge(tile_done[s], turn(s, l, PAIRS["gla"] + it) + 1)
                        e.activation(G[:, bass.ds(2 * it + s, 1), :], PS[s][:, 0:TOK].unsqueeze(1), ACT.Silu)\
                         .then_inc(psum_free[s], 1)
                ac.wait_ge(psum_free[0], turn(0, l, PAIRS["out"]))
                ac.wait_ge(psum_free[1], turn(1, l, PAIRS["out"]))
                ac.wait_ge(pre_dve, (l + 1) * N_PRE_DVE)

                def after_a(i):
                    m = l * NCH + i
                    ac.wait_ge(ac_c, m * len(AC_C) + AC_C.index("g_odd") + 1)
                    e.activation(SQo, Och[:, :, :], ACT.Square).then_inc(ac_p, 1)
                    ac.wait_ge(dv_p, m * len(DV_P) + DV_P.index("yc") + 1)
                    e.activation(SQy, Yc, ACT.Square).then_inc(ac_p, 1)

                def after_b(i):
                    m = l * NCH + i
                    ac.wait_ge(pe_p, m * len(PE_P) + PE_P.index("yvar") + 1)
                    e.activation(SQ[:, 0:NP * C], oE[:, 0:NP * C], ACT.Ln, bias=scal[:, 2:3]).then_inc(ac_p, 1)
                    e.activation(SQ[:, NP * C:], oE[:, NP * C:2 * NP * C], ACT.Ln, bias=scal[:, 0:1]).then_inc(ac_p, 1)
                    ac.wait_ge(ac_p, m * len(AC_P) + AC_P.index("oln") + 1)
                    e.activation(SQ, SQ, ACT.Exp, scale=-0.5).then_inc(ac_p, 1)

                def chunk(i, first):
                    n = l * NCH + i
                    pc = bass.ds(i * CP, CP)

                    def pe(name):
                        ac.wait_ge(pe_c, n * len(PE_C) + PE_C.index(name) + 1)

                    def copy(out, in_):
                        e.activation(out, in_, ACT.Copy).then_inc(ac_c, 1)

                    if not first:
                        ac.wait_ge(po_c, n * len(PO_C))
                    else:
                        ac.wait_ge(st_dve, l * 3 + 1)
                    e.activation(Pp[:, :, :], cum[:, :, pc], ACT.Exp, scale=-KAPPA).then_inc(ac_c, 1)
                    if not first:
                        ac.wait_ge(dv_c, (n - 1) * len(DV_C) + DV_C.index("kt") + 1)
                    e.activation(Pinv[:, :, :], cum[:, :, bass.ds(i * CP + 1, C)], ACT.Exp, scale=KAPPA).then_inc(ac_c, 1)
                    if not first:
                        ac.wait_ge(dv_c, (n - 1) * len(DV_C) + DV_C.index("Sg1") + 1)
                    e.activation(Eg[:, :, :], cg[:, :, bass.ds(i * CP + 1, C)], ACT.Exp, scale=1.0 / 16).then_inc(ac_c, 1)
                    e.activation(Ei[:, :, :], cg[:, :, bass.ds(i * CP + 1, C)], ACT.Exp, scale=-1.0 / 16).then_inc(ac_c, 1)
                    if not first:
                        after_a(i - 1)
                    pe("g_tok")
                    copy(gtok[:, :], oO[:, 0:2 * GDV + 2 * C])
                    if not first:
                        after_b(i - 1)
                    pe("g_out")
                    if not first:
                        ac.wait_ge(dv_p, (n - 1) * len(DV_P) + DV_P.index("on") + 1)
                    o4 = Och[:, :, :].rearrange("p (q h) t -> p q h t", h=2)
                    copy(o4[:, :, 0, :], pair3(oE[:, 0:2 * C]))
                    copy(o4[:, :, 1, :], pair3(oO[:, 0:2 * C]))
                    for X, N in ((0, "A"), (1, "B")):
                        pe("tok" + N)
                        copy(tok[:, X].rearrange("p a q t -> p (a q t)"), pq[X][:, 0:6 * C])
                    for X, N in ((0, "A"), (1, "B")):
                        pe("sq2" + N)
                        copy(sq2[:, X].rearrange("p a q t -> p (a q t)"), tt[X][:, 0:4 * C])
                    for X, N in ((0, "A"), (1, "B")):
                        pe("sq4" + N)
                        copy(sq4[:, X].rearrange("p a q t -> p (a q t)"), pq[X][:, 0:4 * C])
                    for X, N in ((0, "A"), (1, "B")):
                        pe("sq8" + N)
                        copy(sq2[:, X, 0].rearrange("p q t -> p (q t)"), pq[X][:, 0:2 * C])
                    for X, N in ((0, "A"), (1, "B")):
                        pe("F" + N)
                        copy(sq4[:, X].rearrange("p a q t -> p (a q t)"), pq[X][:, 0:4 * C])
                    for X, N in ((0, "A"), (1, "B")):
                        pe("F2" + N)
                        copy(Dm[:, 2 * X:2 * X + 2, :].rearrange("p q t -> p (q t)"), tt[X][:, 0:2 * C])
                    for X, N in ((0, "A"), (1, "B")):
                        pe("Z" + N)
                        copy(Em[:, 2 * X:2 * X + 2, :].rearrange("p q t -> p (q t)"), pq[X][:, 0:2 * C])
                    for X, N in ((0, "A"), (1, "B")):
                        pe("Z1" + N)
                        copy(sq2[:, X, 0].rearrange("p q t -> p (q t)"), tt[X][:, 0:2 * C])
                    for X, N in ((0, "A"), (1, "B")):
                        pe("Y" + N)
                        copy(Ych[:, 2 * X:2 * X + 2, :].rearrange("p q t -> p (q t)"), tt[X][:, 0:2 * C])

                def store_states(c, gla, rwkv):
                    ac.wait_ge(kept, l * 4 + c)
                    for hp in range(2):
                        h = slice(64 * hp, 64 * hp + 64)
                        ac.dma_start(gla[l, 0].rearrange("(q h) d v -> h d q v", h=2)[hp], SgO[h])\
                          .then_inc(states_out, 16)
                        ac.dma_start(rwkv[l, 0].rearrange("(q h) v k -> h v q k", h=2)[hp], StT[h])\
                          .then_inc(states_out, 16)

                chunk(0, True)
                store_states(2, gla_s, rwkv_s)
                with ac.Fori(1, NCH) as i:
                    chunk(i, False)
                after_a(NCH - 1)
                after_b(NCH - 1)

                ac.wait_ge(dv_p, (l + 1) * NCH * len(DV_P))
                ac.wait_ge(po_p, (l + 1) * NCH * len(PO_P))
                store_states(4, gla_p, rwkv_p)
                for k in range(KT):
                    src = G[:, 4 + k, :] if k < 4 else R[:, k - 4, :]
                    e.activation(xh[:, k, :], src, ACT.Copy).then_inc(m_hi, 1)

                for s in range(2):
                    ac.wait_ge(psum_free[s], turn(s, l, PAIRS["ffn"]))
                ac.wait_ge(states_out, (l + 1) * 128)
                norm(l * NORMS + 1)
                norm_hi(l * NORMS + 1)
                ac.wait_ge(n_lo, (l * NORMS + 2) * KT)
                ac.wait_ge(up_pad, l + 1)
                with ac.Fori(0, HALVES) as h:
                    with ac.Fori(0, FT) as it:
                        t = (l * HALVES + h) * FT + it
                        ac.wait_ge(tile_done[0], turn(0, l, PAIRS["ffn"] + h * FFN_PAIRS + it) + 1)
                        ac.wait_ge(f_dve, t * F_STEPS)
                        e.activation(up[:, 2:2 + DEC], PS[0][:, 0:DEC], ACT.Copy)
                        e.activation(up[:, 4 + DEC:4 + TOK], PS[0][:, DEC:TOK], ACT.Copy).then_inc(psum_free[0], 1)
                        ac.wait_ge(f_dve, t * F_STEPS + 6)
                        e.activation(gl[:, :], cv[:, :], ACT.Gelu).then_inc(f_gelu, 1)
                        ac.wait_ge(psum_free[1], turn(1, l, PAIRS["ffn"] + h * FFN_PAIRS + it) + 1)
                        e.activation(hh[:, bass.ds(it, 1), :], hf[:, :].unsqueeze(1), ACT.Copy).then_inc(f_hi, 1)
                ac.wait_ge(rows_turned, l + 1)
                ac.wait_ge(stored, l * 64)
                e.activation(rowout[0:2 * RT, 0, :], PS[3][0:2 * RT, 0:P], ACT.Copy).then_inc(rows_copied, 1)
                e.activation(rowout[0:4 * (F // P), 1, :], PS[3][0:4 * (F // P), P:2 * P], ACT.Copy)\
                 .then_inc(rows_copied, 1)
                ac.wait_ge(rows_copied, 2 * l + 2)
                for g, (sh, co) in enumerate(((shift_s, conv_s), (shift_p, conv_p))):
                    ac.dma_start(sh[l, 0].rearrange("(k p) -> k p", p=P), rowout[g * RT:(g + 1) * RT, 0, :])\
                      .then_inc(stored, 16)
                    n = 2 * (F // P)
                    ac.dma_start(co[l, 0].rearrange("r (k p) -> (r k) p", p=P), rowout[g * n:(g + 1) * n, 1, :])\
                      .then_inc(stored, 16)

            for s in range(2):
                ac.wait_ge(psum_free[s], turn(s, DEPTH, 0, False))
            norm(DEPTH * NORMS)
            for b, (t0, w) in enumerate(BLOCKS):
                ac.wait_ge(y_turned, b + 1)
                if b >= 2:
                    ac.wait_ge(y_stored[b % 2], 16 * (b // 2))
                e.activation(yout[0:w, b % 2, :], PS[b % 2][0:w, :], ACT.Copy).then_inc(y_copied, 1)
                ac.wait_ge(y_copied, b + 1)
                dst = y_sample[0] if b == 0 else y_prompt[0, t0 - DEC:t0 - DEC + w, :]
                ac.dma_start(dst, yout[0:w, b % 2, :]).then_inc(y_stored[b % 2], 16)
            for i in range(2):
                ac.wait_ge(y_stored[i], 16 * ((len(BLOCKS) + 1 - i) // 2))
            ac.wait_ge(stored, 64 * DEPTH)
            ac.wait_ge(states_out, 128 * DEPTH)

        @block.vector
        def _(dv):
            e = nc.vector
            for b, (t0, w) in enumerate(BLOCKS):
                dv.wait_ge(x_turned, b + 1)
                e.tensor_copy(x[:, :, t0:t0 + w], PS[b % 2][:, :].rearrange("p (k t) -> p k t", t=P)[:, :, 0:w])\
                 .then_inc(x_copied, 1)
            dv.wait_ge(consts, N_CONSTS)

            def norm(c, name):
                dv.wait_ge(n_rs, 2 * c + 2)
                for k in range(KT):
                    if k >= 2:
                        dv.wait_ge(n_lo, c * KT + k - 1)
                    e.scalar_tensor_tensor(out=nt[k % 2][:, :], in0=x[:, k, :], scalar=pcol(name, k),
                                           in1=nrs[:, :], op0=ALU.mult, op1=ALU.mult).then_inc(n_t, 1)
                    dv.wait_ge(n_hi, c * KT + k + 1)
                    e.tensor_tensor(xl[:, k, :], nt[k % 2][:, :], xh[:, k, :].bitcast(F32), ALU.subtract)\
                     .then_inc(n_lo, 1)

            with dv.Fori(0, DEPTH) as l:
                dv.wait_ge(par_turned, l + 1)
                e.tensor_copy(par[:, :], PS[3][:, 0:NA + NB]).then_inc(par_ready, 1)
                dv.wait_ge(par_ready, l * 3 + 1)
                e.tensor_scalar(one_ka[:, :], pcol("k_a", 0, NP), -1.0, 1.0, ALU.mult, ALU.add).then_inc(par_ready, 1)
                for p in range(NP):
                    bw = e.tensor_scalar(bonus_w[:, p, :], mean64[:, :], pcol("r_k", p), 64.0, ALU.mult, ALU.mult)
                bw.then_inc(par_ready, 1)
                norm(l * NORMS, "norm_mix")

                mu, shift = ROWS_A["mu"][0], ROWS_A["shift"][0]
                with dv.Fori(0, RT // 2) as it:
                    for s in range(2):
                        j = 2 * it + s
                        t = (l * RT + j) * R_STEPS
                        dv.wait_ge(r_prev, l * RT + j + 1)
                        pv = T[s]
                        e.tensor_copy(last_rows[:, :, bass.ds(j, 1)], pv[:, 64:TOK + 1:SEQ].unsqueeze(2)).then_inc(r_dve, 1)
                        dv.wait_ge(r_dve, t + 1)
                        e.tensor_copy(pv[:, 0:1], par[:, bass.ds(shift + j, 1)]).then_inc(r_dve, 1)
                        e.memset(pv[:, 64:65], 0.0).then_inc(r_dve, 1)
                        dv.wait_ge(r_dve, t + 3)
                        e.tensor_tensor(T[2][:, 0:TOK], pv[:, 0:TOK], PS[s][:, 0:TOK], ALU.subtract).then_inc(r_dve, 1)
                        dv.wait_ge(r_dve, t + 4)
                        e.scalar_tensor_tensor(out=R[:, bass.ds(j, 1), :].squeeze(1), in0=T[2][:, 0:TOK],
                                               scalar=par[:, bass.ds(mu + j, 1)], in1=PS[s][:, 0:TOK],
                                               op0=ALU.mult, op1=ALU.add).then_inc(psum_free[s], 1)

                b = l * N_PRE_DVE
                done = 0

                def step(ins):
                    nonlocal done
                    done += 1
                    ins.then_inc(pre_dve, 1)

                def mine():
                    dv.wait_ge(pre_dve, b + done)

                step(e.memset(cum[:, :, :].rearrange("p a (c t) -> p a c t", t=CP)[:, :, :, 0], 0.0))
                step(e.memset(cg[:, :, :].rearrange("p a (c t) -> p a c t", t=CP)[:, :, :, 0], 0.0))
                assert done == D_ZERO
                for s in range(2):
                    dv.wait_ge(psum_free[s], turn(s, l, PAIRS["gla"], False))
                for p in range(NP):
                    step(e.tensor_scalar(KK[:, p, :], R[:, 4 + p, :], pcol("k_k", p), None, ALU.mult))
                    assert done == D_KK + p
                for p in range(NP):
                    dv.wait_ge(pre_act, l * N_PRE_ACT + A_W + p)
                    step(e.tensor_tensor_scan(cum[:, p, :], restart[:, :], cum[:, p, :], 0.0, ALU.mult, ALU.add))
                for p in range(NP):
                    dv.wait_ge(pre_pe, l * N_PRE_PE + 2 * NP + p + 1)
                    step(e.tensor_scalar(T[p][:, 0:TOK], PS[p][:, 0:TOK], 1e-24 / 64, None, ALU.max))
                    assert done == D_MAX + p
                for p in range(NP):
                    dv.wait_ge(pre_act, l * N_PRE_ACT + A_LN + 2 * p + 1)
                    step(e.tensor_tensor(KK[:, p, :], KK[:, p, :], T[p][:, 0:TOK], ALU.mult))
                    mine()
                    step(e.tensor_scalar(T[p][:, 0:TOK], KA[:, p, :], pcol("k_a", p), one_ka[:, p:p + 1], ALU.mult, ALU.add))
                    mine()
                    step(e.tensor_tensor(R[:, 4 + p, :], R[:, 4 + p, :], T[p][:, 0:TOK], ALU.mult))
                    step(e.tensor_tensor(KA[:, p, :], KK[:, p, :], KA[:, p, :], ALU.mult))
                    mine()
                for q in range(2):
                    dv.wait_ge(pre_pe, l * N_PRE_PE + 3 * NP + q + 1)
                    step(e.tensor_scalar(T[2 * q][:, 0:TOK], PS[2 + q][:, 0:TOK], pcol("gate_b", q), None, ALU.add))
                    mine()
                    step(e.scalar_tensor_tensor(out=T[2 * q + 1][:, 0:TOK], in0=T[2 * q][:, 0:TOK], scalar=-1.0,
                                                in1=T[2 * q][:, 0:TOK], op0=ALU.mult, op1=ALU.max))
                    assert done == D_ABS + 2 * q
                for q in range(2):
                    dv.wait_ge(pre_act, l * N_PRE_ACT + A_GE + 2 * q + 1)
                    v = cg[:, q, :].rearrange("p (c t) -> p c t", t=CP)
                    step(e.scalar_tensor_tensor(out=v[:, :, 1:CP], in0=pair3(T[2 * q][:, 0:TOK]), scalar=0.0,
                                                in1=pair3(T[2 * q + 1][:, 0:TOK]), op0=ALU.min, op1=ALU.subtract))
                    mine()
                    step(e.tensor_tensor_scan(cg[:, q, :], restart[:, :], cg[:, q, :], 0.0, ALU.mult, ALU.add))
                mine()
                assert done == N_PRE_DVE

                dv.wait_ge(st_pe, l * 3 + 1)
                e.tensor_copy(St[:, :, :], pair3(stat[:, 0:NP * C])).then_inc(st_dve, 1)
                dv.wait_ge(states_loaded, (l + 1) * 64)
                for s in range(2):
                    dv.wait_ge(psum_free[s], turn(s, l, PAIRS["out"]))

                def after_a(i):
                    m = l * NCH + i
                    dv.wait_ge(pe_p, m * len(PE_P) + PE_P.index("ymean") + 1)
                    e.scalar_tensor_tensor(out=Yc, in0=pair3(stat[:, 0:NP * C]), scalar=-1.0, in1=Ych[:, :, :],
                                           op0=ALU.mult, op1=ALU.add).then_inc(dv_p, 1)

                def after_b(i):
                    m = l * NCH + i
                    dv.wait_ge(ac_p, m * len(AC_P) + AC_P.index("rstd") + 1)
                    dv.wait_ge(po_p, m * len(PO_P))
                    e.tensor_tensor(Yc, Yc, SQy, ALU.mult).then_inc(dv_p, 1)
                    e.scalar_tensor_tensor(out=On, in0=Och[:, :, :], scalar=pcol("gla_w"), in1=SQo,
                                           op0=ALU.mult, op1=ALU.mult).then_inc(dv_p, 1)

                def after_c(i, cc):
                    m = l * NCH + i
                    dv.wait_ge(po_p, m * len(PO_P) + PO_P.index("yb") + 1)
                    e.tensor_tensor(Yc, Yc, BV, ALU.add).then_inc(dv_p, 1)
                    dv.wait_ge(dv_p, m * len(DV_P) + DV_P.index("ybonus") + 1)
                    e.tensor_tensor(R[:, 0:4, cc], Yc, Gt, ALU.mult).then_inc(dv_p, 1)

                def chunk(i, first):
                    n = l * NCH + i
                    cc = bass.ds(i * C, C)

                    def pe(name):
                        dv.wait_ge(pe_c, n * len(PE_C) + PE_C.index(name) + 1)

                    def act(name):
                        dv.wait_ge(ac_c, n * len(AC_C) + AC_C.index(name) + 1)

                    def mine(name):
                        dv.wait_ge(dv_c, n * len(DV_C) + DV_C.index(name) + 1)

                    def before(sem_, order, name):
                        if not first:
                            dv.wait_ge(sem_, (n - 1) * len(order) + order.index(name) + 1)

                    if not first:
                        after_a(i - 1)
                    act("Ei")
                    e.scalar_tensor_tensor(out=qe[:, :, :], in0=G[:, 0:2, cc], scalar=0.125, in1=Eg[:, :, :],
                                           op0=ALU.mult, op1=ALU.mult).then_inc(dv_c, 1)
                    before(po_c, PO_C, "kd")
                    e.tensor_tensor(ke[:, :, :], G[:, 2:4, cc], Ei[:, :, :], ALU.mult).then_inc(dv_c, 1)
                    before(pe_c, PE_C, "YB")
                    e.scalar_tensor_tensor(out=AR[:, :, 0:C], in0=KK[:, :, cc], scalar=-1.0, in1=Pp[:, :, 0:C],
                                           op0=ALU.mult, op1=ALU.mult).then_inc(dv_c, 1)
                    before(po_c, PO_C, "kh")
                    e.tensor_tensor(Bt[:, :, :], KA[:, :, cc], Pinv[:, :, :], ALU.mult).then_inc(dv_c, 1)
                    e.tensor_tensor(Kt[:, :, :], R[:, 4:8, cc], Pinv[:, :, :], ALU.mult).then_inc(dv_c, 1)
                    pe("g_scores")
                    e.tensor_tensor(scm[:, :, :], pair3(gm[:, 0:2 * C]),
                                    m_si[:, C:2 * C].unsqueeze(1).broadcast_to([P, 2, C]), ALU.mult).then_inc(dv_c, 1)
                    if not first:
                        after_b(i - 1)
                    for X, N in ((0, "A"), (1, "B")):
                        pp = slice(2 * X, 2 * X + 2)
                        pe("gram" + N)
                        e.tensor_tensor(QM[:, pp, :], pair3(pq[X][:, 0:256], P),
                                        m_di[:, :].unsqueeze(1).broadcast_to([P, 2, P]), ALU.mult).then_inc(dv_c, 1)
                        e.tensor_tensor(KM[:, pp, :], pair3(pq[X][:, 256:512], P),
                                        m_si[:, :].unsqueeze(1).broadcast_to([P, 2, P]), ALU.mult).then_inc(dv_c, 1)
                        e.tensor_tensor(Dm[:, pp, :], pair3(tt[X][:, 0:2 * C]),
                                        m_d[:, :].unsqueeze(1).broadcast_to([P, 2, C]), ALU.mult).then_inc(dv_c, 1)
                        e.tensor_tensor(Em[:, pp, :], pair3(tt[X][:, 0:2 * C]),
                                        m_e[:, :].unsqueeze(1).broadcast_to([P, 2, C]), ALU.mult).then_inc(dv_c, 1)
                        mine("Q" + N)
                        e.tensor_tensor(Ta[:, pp, :], QM[:, pp, 0:C], ident2[:, :].unsqueeze(1).broadcast_to([P, 2, C]),
                                        ALU.add).then_inc(dv_c, 1)
                    if not first:
                        after_c(i - 1, bass.ds((i - 1) * C, C))
                    pe("g_state")
                    for q in range(2):
                        e.scalar_tensor_tensor(out=Sg[:, q, :], in0=Sg[:, q, :], scalar=Eg[:, q, C - 1:C],
                                               in1=gm[:, q * GDV:(q + 1) * GDV], op0=ALU.mult, op1=ALU.add)\
                         .then_inc(dv_c, 1)
                    for step_, src, dst in (("T2", Ta, Tb), ("T4", Tb, Ta), ("T8", Ta, Tb)):
                        for X, N in ((0, "A"), (1, "B")):
                            pp = slice(2 * X, 2 * X + 2)
                            pe(step_ + N)
                            e.tensor_tensor(dst[:, pp, :], src[:, pp, :], pair3(tt[X][:, 0:2 * C]), ALU.add)\
                             .then_inc(dv_c, 1)
                    for X, N in ((0, "A"), (1, "B")):
                        pe("Z2" + N)
                        e.tensor_tensor(sq2[:, X, 1], sq2[:, X, 0], pair3(pq[X][:, 0:2 * C]), ALU.add).then_inc(dv_c, 1)
                    for X, N in ((0, "A"), (1, "B")):
                        pe("U" + N)
                        mine("Z2" + N)
                        e.tensor_tensor(Ta[:, 2 * X:2 * X + 2, :], sq2[:, X, 1], pair3(tt[X][:, 0:2 * C]), ALU.add)\
                         .then_inc(dv_c, 1)
                    dv.wait_ge(po_c, n * len(PO_C) + PO_C.index("stp") + 1)
                    for X, N in ((0, "A"), (1, "B")):
                        pp = slice(2 * X, 2 * X + 2)
                        pe("S" + N)
                        e.tensor_tensor(St[:, pp, :], StP[:, pp, :], pair3(pq[X][:, 0:2 * C]), ALU.add)\
                         .then_inc(dv_c, 1)
                    pe("bonus")
                    e.tensor_tensor(BV, pair3(stat[:, 0:NP * C]), R[:, 8:12, cc], ALU.mult).then_inc(dv_c, 1)
                    e.tensor_copy(Gt, pair3(stat[:, NP * C:2 * NP * C])).then_inc(dv_c, 1)

                def keep_states(c, i):
                    dv.wait_ge(st_pe, l * 3 + c)
                    dv.wait_ge(dv_c, (l * NCH + i + 1) * len(DV_C))
                    e.tensor_copy(SgO, Sg[:, :, :]).then_inc(kept, 1)
                    e.tensor_copy(StT, pair3(stat[:, 0:NP * C])).then_inc(kept, 1)

                chunk(0, True)
                keep_states(2, 0)
                dv.wait_ge(kept, l * 4 + 2)
                dv.wait_ge(pe_c, (l * NCH + 1) * len(PE_C))
                e.memset(Sg[:, :, :], 0.0).then_inc(st_dve, 1)
                e.memset(St[:, :, :], 0.0).then_inc(st_dve, 1)
                with dv.Fori(1, NCH) as i:
                    chunk(i, False)
                after_a(NCH - 1)
                after_b(NCH - 1)
                after_c(NCH - 1, bass.ds((NCH - 1) * C, C))
                dv.wait_ge(states_out, l * 128 + 64)
                keep_states(3, NCH - 1)

                for k in range(KT):
                    src = G[:, 4 + k, :] if k < 4 else R[:, k - 4, :]
                    dv.wait_ge(m_hi, l * KT + k + 1)
                    e.tensor_tensor(xl[:, k, :], src, xh[:, k, :].bitcast(F32), ALU.subtract).then_inc(m_lo, 1)
                dv.wait_ge(states_out, (l + 1) * 128)
                apart(dv)

                def add_tile(s, k, t):
                    xt = x[:, bass.ds(t, 1), :].squeeze(1)
                    dv.wait_ge(tile_done[s], k + 1)
                    return e.tensor_tensor(xt, xt, PS[s][:, 0:TOK], ALU.add)

                with dv.Fori(0, KT // 2) as it:
                    for s in range(2):
                        k = turn(s, l, PAIRS["out"] + it)
                        add_tile(s, k, 2 * it + s).then_inc(psum_free[s], 1)
                norm(l * NORMS + 1, "norm_ffn")

                e.memset(up[:, 2 + DEC:4 + DEC], 0.0).then_inc(up_pad, 1)
                cw, cb, cache = NA + ROWS_B["conv_w"][0], NA + ROWS_B["conv_b"][0], ROWS_A["cache"][0]
                FF = F // P
                with dv.Fori(0, HALVES) as h:
                    with dv.Fori(0, FT) as it:
                        t = (l * HALVES + h) * FT + it
                        f = h * FT + it
                        q = t * F_STEPS

                        def mine(c):
                            dv.wait_ge(f_dve, q + c)

                        mine(0)
                        e.tensor_copy(up[:, 0:2].unsqueeze(2),
                                      par[:, cache:cache + 2 * FF].rearrange("p (r k) -> p r k", r=2)[:, :, bass.ds(f, 1)])\
                         .then_inc(f_dve, 1)
                        dv.wait_ge(psum_free[0], turn(0, l, PAIRS["ffn"] + h * FFN_PAIRS + it) + 1)
                        mine(1)
                        e.tensor_scalar(cv[:, :], up[:, 0:2 + TOK], par[:, bass.ds(cw + f, 1)], par[:, bass.ds(cb + f, 1)],
                                        ALU.mult, ALU.add).then_inc(f_dve, 1)
                        for r in range(2):
                            e.tensor_copy(last_conv[:, r:4:2, bass.ds(f, 1)],
                                          up[:, 64 + r:580:SEQ + 2].unsqueeze(2)).then_inc(f_dve, 1)
                        mine(2)
                        e.scalar_tensor_tensor(out=cv[:, :], in0=up[:, 1:3 + TOK], scalar=par[:, bass.ds(cw + FF + f, 1)],
                                               in1=cv[:, :], op0=ALU.mult, op1=ALU.add).then_inc(f_dve, 1)
                        mine(5)
                        e.scalar_tensor_tensor(out=cv[:, :], in0=up[:, 2:4 + TOK], scalar=par[:, bass.ds(cw + 2 * FF + f, 1)],
                                               in1=cv[:, :], op0=ALU.mult, op1=ALU.add).then_inc(f_dve, 1)
                        dv.wait_ge(tile_done[1], turn(1, l, PAIRS["ffn"] + h * FFN_PAIRS + it) + 1)
                        dv.wait_ge(f_gelu, t + 1)
                        e.tensor_tensor(hf[:, 0:DEC], gl[:, 0:DEC], PS[1][:, 0:DEC], ALU.mult).then_inc(f_dve, 1)
                        e.tensor_tensor(hf[:, DEC:TOK], gl[:, DEC + 2:TOK + 2], PS[1][:, DEC:TOK], ALU.mult)\
                         .then_inc(psum_free[1], 1)
                        dv.wait_ge(f_hi, t + 1)
                        e.tensor_tensor(hl[:, bass.ds(it, 1), :].squeeze(1), hf[:, :],
                                        hh[:, bass.ds(it, 1), :].squeeze(1).bitcast(F32), ALU.subtract)\
                         .then_inc(f_dve, 1)
                    with dv.Fori(0, KT // 2) as it:
                        for s in range(2):
                            k = turn(s, l, PAIRS["ffn"] + h * FFN_PAIRS + FT + it)
                            add_tile(s, k, 2 * it + s).then_inc(psum_free[s], 1)

            c = DEPTH * NORMS
            dv.wait_ge(n_rs, 2 * c + 2)
            for k in range(KT):
                e.scalar_tensor_tensor(out=x[:, k, :], in0=x[:, k, :], scalar=pcol("norm_final", k),
                                       in1=nrs[:, :], op0=ALU.mult, op1=ALU.mult).then_inc(n_t, 1)


_INS = ["x_prompt", "x_sample", "state_gla", "state_rwkv", "state_rwkv_shift", "cache_ffn_conv",
        "norm_mix", "w_in", "gla_gate_w2", "gla_gate_b", "gla_norm_w", "rwkv_mu", "rwkv_w0", "rwkv_w2",
        "rwkv_a0", "rwkv_a2", "rwkv_g2", "rwkv_k_k", "rwkv_k_a", "rwkv_r_k", "rwkv_ln_w", "rwkv_ln_b",
        "w_out", "norm_ffn", "ffn_w_up", "ffn_conv_w", "ffn_conv_b", "ffn_w_down", "norm_final"]
_STATES = [(DEPTH, 1, GH, GDK, GDV), (DEPTH, 1, RC // RN, RN, RN), (DEPTH, 1, RWKV_COLS), (DEPTH, 1, 2, F)]
_OUTS = [(1, SEQ, D), (1, DEC, D)] + _STATES + _STATES


def kernel(**inputs):
    import numpy as np
    import concourse.bacc as bacc
    from concourse.bass_utils import run_bass_kernel_spmd as run

    nc = bacc.Bacc("TRN2", target_bir_lowering=False, num_devices=1)
    arrays, args = {}, []
    for name in _INS:
        a = np.ascontiguousarray(inputs[name])
        arrays[f"in_{name}"] = a
        args.append(nc.dram_tensor(f"in_{name}", a.shape, mybir.dt.from_np(a.dtype), kind="ExternalInput").ap())
    for i, shape in enumerate(_OUTS):
        args.append(nc.dram_tensor(f"out_{i}", shape, F32, kind="ExternalOutput").ap())
    program(nc, *args)
    r = run(nc, [arrays], core_ids=[0])
    return tuple(r.results[0][f"out_{i}"] for i in range(len(_OUTS)))
```

```python
from contextlib import ExitStack

import concourse.bass as bass
from concourse import mybir

F32 = mybir.dt.float32
F32R = mybir.dt.float32r
BF16 = mybir.dt.bfloat16
ALU = mybir.AluOpType
ACT = mybir.ActivationFunctionType

P = 128
D = 1024
SEQ = 512
DEC = 64
DEPTH = 2
TOK = SEQ + DEC
C = 64
HT = TOK // 2
NCH = TOK // C
KT = D // P
GH, GDV = 4, 128
GDK = 64
GK, GV = GH * GDK, GH * GDV
RC, RN = 512, 64
NP = RC // P
GLA_COLS = 2 * GK + 2 * GV + 16
RWKV_COLS = 3 * RC + 256
RT = RWKV_COLS // P
GT = (2 * GK + 2 * GV) // P
LR_AT = 96
F = 2816
HALVES = 2
FT = F // P // HALVES
CP = C + 1
EPS = 1e-6
GN_EPS = 64e-5
KAPPA = 0.6065306597126334
LN2 = 0.6931471805599453

ROWS_A, ROWS_B = {}, {}
_n = 0
for _name, _count in (("norm_mix", 8), ("norm_ffn", 8), ("norm_final", 8), ("gate_b", 2), ("gla_w", 1),
                      ("mu", RT), ("w0", 4), ("a0", 4), ("k_k", 4), ("k_a", 4), ("r_k", 4),
                      ("ln_w", 4), ("ln_b", 4), ("shift", RT), ("cache", 44)):
    ROWS_A[_name] = (_n, _count)
    _n += _count
NA = _n
_n = 0
for _name, _count in (("conv_w", 66), ("conv_b", 22)):
    ROWS_B[_name] = (_n, _count)
    _n += _count
NB = _n

PAIRS = dict(rwkv=0, gla=RT // 2, out=RT // 2 + GT // 2, ffn=RT // 2 + GT // 2 + KT // 2)
FFN_PAIRS = FT + KT // 2
PAIRS_OF_LAYER = PAIRS["ffn"] + HALVES * FFN_PAIRS


N_ROWS = 17
A_TANH, A_W, A_A, A_SQ, A_LN, A_GE, N_PRE_ACT = 1, 3, 7, 11, 15, 23, 26
D_ZERO, D_KK, D_MAX, D_ABS, N_PRE_DVE = 2, 3, 11, 32, 38
N_PRE_PE = 14
F_STEPS = 9
R_STEPS = 4
N_CONSTS = 46


def turn(s, l, pair, after_lowrank=True):
    if s == 0:
        return l * (PAIRS_OF_LAYER + 1) + pair + (1 if after_lowrank else 0)
    return l * PAIRS_OF_LAYER + pair


PE_C = ["g_scores", "g_tok", "gramA", "gramB", "g_out", "g_state", "tokA", "tokB",
        "D2A", "D2B", "D4A", "T2A", "D4B", "T2B", "D8A", "T4A", "D8B", "T4B",
        "D16A", "T8A", "D16B", "T8B", "T16A", "T16B",
        "ZA", "ZB", "Z1A", "Z1B", "Z2A", "Z2B", "UA", "UB", "YA", "SA", "YB", "SB", "bonus"]
AC_C = ["P", "Pinv", "Eg", "Ei", "g_tok", "g_o", "tokA", "tokB", "D2A", "D2B",
        "D4A", "D4B", "D8A", "D8B", "D16A", "D16B", "ZA", "ZB", "Z1A", "Z1B", "UA", "UB", "YA", "YB"]
DV_C = ["qe0", "qe1", "ke", "at", "bt0", "bt1", "kt0", "kt1", "g_scores0", "g_scores1", "DA", "EA", "TA", "QA", "KA", "XA",
        "DB", "EB", "TB", "QB", "KB", "XB",
        "Sg0", "Sg1", "T2A", "T2B", "T4A", "T4B", "T8A", "T8B", "T16A", "T16B", "Z2A", "Z2B",
        "StA", "StB", "bonus", "gate"]
PO_C = ["rt", "vs", "vgs", "kd", "bh0", "bh1", "kh0", "kh1", "stp", "rk1", "rk"]
PE_P = ["ymean", "orms", "yvar"]
AC_P = ["osq", "ysq", "yln", "oln", "rstd"]
DV_P = ["yc", "yn", "on", "ybonus", "y"]
PO_P = ["yw", "yb", "o"]


def program(nc, x_prompt, x_sample, state_gla, state_rwkv, state_rwkv_shift, cache_ffn_conv,
            norm_mix, w_in, gla_gate_w2, gla_gate_b, gla_norm_w, rwkv_mu, rwkv_w0, rwkv_w2,
            rwkv_a0, rwkv_a2, rwkv_g2, rwkv_k_k, rwkv_k_a, rwkv_r_k, rwkv_ln_w, rwkv_ln_b,
            w_out, norm_ffn, ffn_w_up, ffn_conv_w, ffn_conv_b, ffn_w_down, norm_final,
            y_prompt, y_sample, gla_p, rwkv_p, shift_p, conv_p, gla_s, rwkv_s, shift_s, conv_s):
    with ExitStack() as ctx:
        def sb(name, shape, dt=F32, scope=ctx):
            return scope.enter_context(nc.sbuf_tensor(name, shape, dt))

        def sem(name):
            return ctx.enter_context(nc.semaphore(name))

        x = sb("x", [P, KT, TOK])
        ident = sb("ident", [P, P])
        ident2 = sb("ident2", [P, C])
        mean128 = sb("mean128", [P, P])
        mean64 = sb("mean64", [P, P])
        m_bd = sb("m_bd", [P, P])
        m_be = sb("m_be", [P, P])
        m_si = sb("m_si", [P, P])
        m_et = sb("m_et", [P, C])
        restart = sb("restart", [P, NCH * CP], BF16)
        rows_a = sb("rows_a", [NA, P])
        rows_b = sb("rows_b", [NB, P])
        par = sb("par", [P, NA + NB])
        scal = sb("scal", [P, 3])
        rowout = sb("rowout", [P, 2, P])
        one_ka = sb("one_ka", [P, NP])
        w2a2 = sb("w2a2", [P, RC])
        g2 = sb("g2", [P, RC])
        gw2 = sb("gw2", [P, GK])
        r_k64 = sb("r_k64", [P, NP])
        Tt = sb("Tt", [P, 2, 2, P])
        last_rows = sb("last_rows", [P, 2, RT])
        last_conv = sb("last_conv", [P, 4, F // P])
        raw = [sb(f"raw{s}", [P, FT * P]) for s in range(2)]
        whi = [sb(f"whi{s}", [P, FT * P], F32R) for s in range(2)]
        wlo = [sb(f"wlo{s}", [P, FT * P], F32R) for s in range(2)]
        T = [sb(f"T{i}", [P, 580]) for i in range(4)]
        with ExitStack() as s1:
            xh = sb("xh", [P, KT, TOK], F32R, s1)
            xl = sb("xl", [P, KT, TOK], F32R, s1)
        work = sb("work", [P, 2 * KT * TOK])
        taken = 0

        def cut(shape):
            nonlocal taken
            sizes, n = shape[1:], 1
            for size in sizes:
                n *= size
            piece = work[:, taken:taken + n]
            taken += n
            assert taken <= 2 * KT * TOK
            names = "abcd"[:len(sizes)]
            return piece.rearrange(f"p ({' '.join(names)}) -> p {' '.join(names)}",
                                   **dict(zip(names[1:], sizes[1:])))

        Pp = cut([P, NP, CP])
        Pinv = cut([P, NP, C])
        AR = cut([P, NP, 2 * C])
        Bt = cut([P, NP, P])
        Kt = cut([P, NP, P])
        Bh = cut([P, NP, C])
        Kh = cut([P, NP, C])
        Vs = cut([P, NP, C])
        QM = cut([P, NP, C])
        KM = cut([P, NP, 2 * C])
        Et = cut([P, NP, C])
        DE = [cut([P, 2, 2, 2, P]) for _ in range(2)]
        tail = DE[1].rearrange("p x d q t -> p (x d q t)")
        Z, Z1, W, U = (tail[:, j * NP * C:(j + 1) * NP * C].rearrange("p (a b) -> p a b", b=C) for j in range(4))
        tok = cut([P, 2, 3, 2, C])
        St = cut([P, NP, C])
        Ych = cut([P, NP, C])
        Sg = cut([P, 2, GDV])
        Eg = cut([P, 2, C])
        Ei = cut([P, 2, C])
        qe = cut([P, 2, P])
        ke = cut([P, 2, C])
        kd = cut([P, 2, C])
        Vgs = cut([P, GH, C])
        gtok = cut([P, 2 * GDV + 2 * C])
        Och = cut([P, GH, C])
        StP = raw[0][:, KT * P:KT * P + NP * C].rearrange("p (a b) -> p a b", b=C)
        rk = raw[1][:, KT * P:KT * P + NP * C].rearrange("p (a b) -> p a b", b=C)
        scm = T[3][:, NP * C:2 * NP * C].rearrange("p (a b) -> p a b", b=P)
        Yc = T[0][:, 0:NP * C].rearrange("p (a b) -> p a b", b=C)
        On = T[0][:, NP * C:2 * NP * C].rearrange("p (a b) -> p a b", b=C)
        SQ = T[1][:, 0:2 * NP * C]
        SQy = T[1][:, 0:NP * C].rearrange("p (a b) -> p a b", b=C)
        SQo = T[1][:, NP * C:2 * NP * C].rearrange("p (a b) -> p a b", b=C)
        BV = T[2][:, 0:NP * C].rearrange("p (a b) -> p a b", b=C)
        Gt = T[2][:, NP * C:2 * NP * C].rearrange("p (a b) -> p a b", b=C)
        Sraw = T[3][:, 0:NP * C].rearrange("p (a b) -> p a b", b=C)
        nsq = [T[i][:, 0:TOK] for i in range(2)]
        nacc = T[2][:, 0:TOK]
        with ExitStack() as s2:
            hh = sb("hh", [P, FT, TOK], F32R, s2)
            hl = sb("hl", [P, FT, TOK], F32R, s2)
            up = sb("up", [P, 4 + TOK], scope=s2)
            cv = sb("cv", [P, 2 + TOK], scope=s2)
            gl = sb("gl", [P, 2 + TOK], scope=s2)
            hf = sb("hf", [P, TOK], scope=s2)
        with ExitStack() as s2:
            xin = sb("xin", [P, 5, D], scope=s2)
            yout = sb("yout", [P, 2, D], scope=s2)
            nln = sb("nln", [P, TOK], scope=s2)
            nrs = sb("nrs", [P, TOK], scope=s2)
            nt = [sb(f"nt{i}", [P, TOK], scope=s2) for i in range(2)]
        R = sb("R", [P, RT, TOK])
        KK = sb("KK", [P, NP, TOK])
        KA = sb("KA", [P, NP, TOK])
        cum = sb("cum", [P, NP, NCH * CP])
        G = sb("G", [P, GT, TOK])
        cg = sb("cg", [P, 2, NCH * CP])
        SgO = R[:, 12, 0:2 * GDV].rearrange("p (a b) -> p a b", b=GDV)
        StT = R[:, 12, 2 * GDV:2 * GDV + NP * C].rearrange("p (a b) -> p a b", b=C)

        PS = [ctx.enter_context(nc.psum_tensor(f"ps{i}", [P, 1024], F32)) for i in range(4)]

        def bank(b):
            return PS[b // 2][:, 512 * (b % 2):512 * (b % 2) + 512]

        pq = [bank(0), bank(2)]
        tt = [bank(1), bank(3)]
        gm, oE, oO, stat = bank(4), bank(5), bank(6), bank(7)
        nsum = PS[2]

        def acc(t):
            return t.rearrange("p (b t) -> p b t", t=512)[:, :, 0:HT]

        def by_half(ap):
            return ap.rearrange("p (b t) -> p b t", t=HT)

        def pair3(ap, n=C):
            return ap.rearrange("p (a b) -> p a b", b=n)

        def pcol(name, j=0, n=1):
            at, _ = ROWS_A[name] if name in ROWS_A else (NA + ROWS_B[name][0], 0)
            return par[:, at + j:at + j + n]

        x_loaded = sem("x_loaded")
        rows_loaded = sem("rows_loaded")
        small_loaded = sem("small_loaded")
        states_loaded = sem("states_loaded")
        w_loaded = [sem(f"w_loaded{s}") for s in range(2)]
        w_hi = [sem(f"w_hi{s}") for s in range(2)]
        w_lo = [sem(f"w_lo{s}") for s in range(2)]
        tile_done = [sem(f"tile_done{s}") for s in range(2)]
        psum_free = [sem(f"psum_free{s}") for s in range(2)]
        consts = sem("consts")
        x_turned = sem("x_turned")
        x_copied = sem("x_copied")
        par_turned = sem("par_turned")
        par_ready = sem("par_ready")
        n_sq = sem("n_sq")
        n_acc = sem("n_acc")
        n_sum = sem("n_sum")
        n_rs = sem("n_rs")
        n_t = sem("n_t")
        n_hi = sem("n_hi")
        n_lo = sem("n_lo")
        r_prev = sem("r_prev")
        r_dve = sem("r_dve")
        pre_pe = sem("pre_pe")
        pre_act = sem("pre_act")
        pre_dve = sem("pre_dve")
        st_pe = sem("st_pe")
        st_dve = sem("st_dve")
        pe_c, ac_c, dv_c, po_c = sem("pe_c"), sem("ac_c"), sem("dv_c"), sem("po_c")
        pe_p, ac_p, dv_p, po_p = sem("pe_p"), sem("ac_p"), sem("dv_p"), sem("po_p")
        m_hi = sem("m_hi")
        m_lo = sem("m_lo")
        up_pad = sem("up_pad")
        f_dve, f_gelu, f_hi = sem("f_dve"), sem("f_gelu"), sem("f_hi")
        cleared = sem("cleared")
        kept = sem("kept")
        waited = sem("waited")
        states_out = sem("states_out")
        rows_turned, rows_copied = sem("rows_turned"), sem("rows_copied")
        y_turned, y_copied = sem("y_turned"), sem("y_copied")
        stored = sem("stored")
        y_stored = [sem(f"y_stored{i}") for i in range(2)]

        def apart(engine):
            engine.sem_inc(waited)

        block = ctx.enter_context(nc.Block())
        NORMS = 2
        BLOCKS = [(0, DEC)] + [(DEC + P * b, P) for b in range(SEQ // P)]

        @block.sync
        def _(sp):
            sp.dma_start(xin[0:DEC, 0, :], x_sample[0]).then_inc(x_loaded, 16)
            sp.dma_start(xin[:, 1:5, :], x_prompt[0].rearrange("(b p) d -> p b d", p=P)).then_inc(x_loaded, 16)
            with sp.Fori(0, DEPTH) as l:
                def rows(name, src):
                    t, o, n = (rows_a, *ROWS_A[name]) if name in ROWS_A else (rows_b, *ROWS_B[name])
                    sp.dma_start(t[o:o + n, :], src).then_inc(rows_loaded, 16)

                sp.wait_ge(par_turned, l)
                rows("norm_mix", norm_mix[l].rearrange("(k p) -> k p", p=P))
                rows("norm_ffn", norm_ffn[l].rearrange("(k p) -> k p", p=P))
                rows("norm_final", norm_final.rearrange("(k p) -> k p", p=P))
                rows("gate_b", gla_gate_b[l].rearrange("(k p) -> k p", p=P))
                rows("gla_w", gla_norm_w[l].rearrange("(k p) -> k p", p=P))
                rows("mu", rwkv_mu[l].rearrange("(k p) -> k p", p=P))
                for name, src in (("w0", rwkv_w0), ("a0", rwkv_a0), ("k_k", rwkv_k_k), ("k_a", rwkv_k_a),
                                  ("ln_w", rwkv_ln_w), ("ln_b", rwkv_ln_b)):
                    rows(name, src[l].rearrange("(k p) -> k p", p=P))
                rows("r_k", rwkv_r_k[l].rearrange("(k h) n -> k (h n)", h=2))
                rows("shift", state_rwkv_shift[l, 0].rearrange("(k p) -> k p", p=P))
                rows("cache", cache_ffn_conv[l, 0].rearrange("r (k p) -> (r k) p", p=P))
                rows("conv_w", ffn_conv_w[l].rearrange("r (k p) -> (r k) p", p=P))
                rows("conv_b", ffn_conv_b[l].rearrange("(k p) -> k p", p=P))

                def load(s, k, dst, src):
                    sp.wait_ge(w_lo[s], k)
                    sp.dma_start(dst, src).then_inc(w_loaded[s], 16)

                def in_tile(s, k, col):
                    load(s, k, raw[s][:, 0:KT * P].rearrange("p (k m) -> p k m", m=P),
                         w_in[l].rearrange("(k p) c -> p k c", p=P)[:, :, bass.ds(col, P)])

                with sp.Fori(0, RT // 2) as it:
                    for s in range(2):
                        in_tile(s, turn(s, l, PAIRS["rwkv"] + it, False), GLA_COLS + (2 * it + s) * P)
                sp.wait_ge(consts, N_CONSTS)
                sp.dma_start(w2a2[0:64, :], rwkv_w2[l]).then_inc(small_loaded, 16)
                sp.dma_start(w2a2[64:128, :], rwkv_a2[l]).then_inc(small_loaded, 16)
                sp.dma_start(g2[:, :], rwkv_g2[l]).then_inc(small_loaded, 16)
                sp.dma_start(gw2[LR_AT:LR_AT + 16, :], gla_gate_w2[l]).then_inc(small_loaded, 16)
                in_tile(0, turn(0, l, PAIRS["gla"], False), GLA_COLS - 16 - LR_AT)
                with sp.Fori(0, GT // 2) as it:
                    for s in range(2):
                        in_tile(s, turn(s, l, PAIRS["gla"] + it), (2 * it + s) * P)
                def out_pair(it):
                    for s in range(2):
                        load(s, turn(s, l, PAIRS["out"] + it), raw[s][:, 0:KT * P].rearrange("p (k m) -> p k m", m=P),
                             w_out[l].rearrange("(k p) c -> p k c", p=P)[:, :, bass.ds((2 * it + s) * P, P)])

                out_pair(0)
                sp.wait_ge(tile_done[0], turn(0, l, PAIRS["out"]))
                sp.wait_ge(tile_done[1], turn(1, l, PAIRS["out"]))
                sp.wait_ge(pre_dve, (l + 1) * N_PRE_DVE)
                for hp in range(2):
                    h = slice(64 * hp, 64 * hp + 64)
                    sp.dma_start(Sg[h, :, :], state_gla[l, 0].rearrange("(q h) d v -> h d q v", h=2)[hp])\
                      .then_inc(states_loaded, 16)
                    sp.dma_start(Sraw[h, :, :], state_rwkv[l, 0].rearrange("(q h) v k -> h v q k", h=2)[hp])\
                      .then_inc(states_loaded, 16)
                with sp.Fori(1, KT // 2) as it:
                    out_pair(it)
                with sp.Fori(0, HALVES) as h:
                    with sp.Fori(0, FT) as it:
                        for s in range(2):
                            load(s, turn(s, l, PAIRS["ffn"] + h * FFN_PAIRS + it),
                                 raw[s][:, 0:KT * P].rearrange("p (k m) -> p k m", m=P),
                                 ffn_w_up[l].rearrange("(k p) c -> p k c", p=P)[:, :, bass.ds(s * F + (h * FT + it) * P, P)])
                    with sp.Fori(0, KT // 2) as it:
                        for s in range(2):
                            load(s, turn(s, l, PAIRS["ffn"] + h * FFN_PAIRS + FT + it),
                                 raw[s][:, :].rearrange("p (k m) -> p k m", m=P),
                                 ffn_w_down[l].rearrange("(g k p) c -> g p k c", p=P, g=HALVES)[h][:, :, bass.ds((2 * it + s) * P, P)])

        @block.gpsimd
        def _(po):
            e = nc.gpsimd
            n = 0

            def const(ins):
                nonlocal n
                n += 1
                ins.then_inc(consts, 1)
                po.wait_ge(consts, n)

            def keep(out, pattern, base, mult):
                const(e.affine_select(out=out, in_=out, compare_op=ALU.is_ge, fill=0.0, base=base,
                                      pattern=pattern, channel_multiplier=mult))

            const(e.memset(ident[:, :], 1.0))
            keep(ident[:, :], [[1, P]], 0, -1)
            keep(ident[:, :], [[-1, P]], 0, 1)
            for j, value in enumerate((EPS, 10 * LN2, GN_EPS)):
                const(e.memset(scal[:, j:j + 1], value))
            const(e.memset(mean128[:, :], 1.0 / 128))
            const(e.memset(mean64[:, :], 0.0))
            for m in (m_bd, m_be):
                const(e.memset(m[:, :], 0.0))
            for m in (ident2, m_si, m_et):
                const(e.memset(m[:, :], 1.0))
            const(e.memset(restart[:, :], 1.0))
            const(e.memset(restart[:, :].rearrange("p (c t) -> p c t", t=CP)[:, :, 0:1], 0.0))
            const(e.memset(gw2[:, :], 0.0))
            for hp in range(2):
                h = slice(64 * hp, 64 * hp + 64)
                const(e.memset(mean64[h, 64 * hp:64 * hp + 64], 1.0 / 64))
                keep(ident2[h, :], [[1, C]], 0, -1)
                keep(ident2[h, :], [[-1, C]], 0, 1)
                keep(m_si[h, C:2 * C], [[1, C]], 0, -1)
                keep(m_si[h, 0:C], [[1, C]], -1, -1)
                for m, step, sign in ((m_bd, -1, 1), (m_be, 1, -1)):
                    own = m[h, 64 * hp:64 * hp + 64]
                    const(e.memset(own, 1.0))
                    keep(own, [[step, C]], -1, sign)
                    v = own.rearrange("p (b j) -> p b j", j=32)
                    keep(v, [[-32, 2], [0, 32]], 0, 1)
                    keep(v, [[32, 2], [0, 32]], 31, -1)
                keep(m_et[h, :], [[0, C]], 31, -1)
                keep(m_et[h, :], [[1, C]], -32, 0)

            def split(s, k, width):
                po.wait_ge(w_hi[s], k + 1)
                e.tensor_tensor(wlo[s][:, 0:width], raw[s][:, 0:width], whi[s][:, 0:width].bitcast(F32),
                                ALU.subtract).then_inc(w_lo[s], 1)

            assert n == N_CONSTS, n
            with po.Fori(0, DEPTH) as l:
                with po.Fori(0, RT // 2) as it:
                    for s in range(2):
                        split(s, turn(s, l, PAIRS["rwkv"] + it, False), KT * P)
                split(0, turn(0, l, PAIRS["gla"], False), KT * P)
                with po.Fori(0, GT // 2) as it:
                    for s in range(2):
                        split(s, turn(s, l, PAIRS["gla"] + it), KT * P)
                for s in range(2):
                    split(s, turn(s, l, PAIRS["out"]), KT * P)

                def after(i, cc):
                    m = l * NCH + i
                    po.wait_ge(dv_p, m * len(DV_P) + DV_P.index("yn") + 1)
                    e.tensor_tensor(Yc, Yc, pcol("ln_w", 0, NP).unsqueeze(2).broadcast_to([P, NP, C]), ALU.mult)\
                     .then_inc(po_p, 1)
                    po.wait_ge(po_p, m * len(PO_P) + 1)
                    e.tensor_tensor(Yc, Yc, pcol("ln_b", 0, NP).unsqueeze(2).broadcast_to([P, NP, C]), ALU.add)\
                     .then_inc(po_p, 1)
                    po.wait_ge(dv_p, m * len(DV_P) + DV_P.index("on") + 1)
                    e.tensor_tensor(G[:, 4:8, cc], On, G[:, 8:12, cc], ALU.mult).then_inc(po_p, 1)

                def chunk(i, first):
                    n = l * NCH + i
                    cc = bass.ds(i * C, C)

                    def mine(name):
                        po.wait_ge(po_c, n * len(PO_C) + PO_C.index(name) + 1)

                    def act(name):
                        po.wait_ge(ac_c, n * len(AC_C) + AC_C.index(name) + 1)

                    def dve(name):
                        po.wait_ge(dv_c, n * len(DV_C) + DV_C.index(name) + 1)

                    if not first:
                        po.wait_ge(pe_c, (n - 1) * len(PE_C) + PE_C.index("YB") + 1)
                    else:
                        for s in range(2):
                            po.wait_ge(psum_free[s], turn(s, l, PAIRS["out"]))
                    act("P")
                    e.tensor_tensor(AR[:, :, C:2 * C], R[:, 0:4, cc], Pp[:, :, 1:CP], ALU.mult).then_inc(po_c, 1)
                    e.tensor_copy(Vs[:, :, :], R[:, 8:12, cc]).then_inc(po_c, 1)
                    e.tensor_copy(Vgs[:, :, :], G[:, 4:8, cc]).then_inc(po_c, 1)
                    dve("ke")
                    act("Eg")
                    e.tensor_tensor(kd[:, :, :], ke[:, :, :], Eg[:, :, C - 1:C].broadcast_to([P, 2, C]), ALU.mult)\
                     .then_inc(po_c, 1)
                    last = Pp[:, :, C:CP].broadcast_to([P, NP, C])
                    before = "kd"
                    for dst, src, name in ((Bh, Bt, "bt1"), (Kh, Kt, "kt1")):
                        dve(name)
                        for hp in range(2):
                            h = slice(64 * hp, 64 * hp + 64)
                            mine(before)
                            before = PO_C[PO_C.index(before) + 1]
                            e.tensor_tensor(dst[h, :, :], src[h, :, h], last[h], ALU.mult).then_inc(po_c, 1)
                    mine(before)
                    if not first:
                        po.wait_ge(dv_c, (n - 1) * len(DV_C) + DV_C.index("StB") + 1)
                    po.wait_ge(st_dve, l * 3 + (1 if first else 3))
                    e.tensor_tensor(StP[:, :, :], St[:, :, :], last, ALU.mult).then_inc(po_c, 1)
                    if not first:
                        po.wait_ge(pe_c, (n - 1) * len(PE_C) + PE_C.index("bonus") + 1)
                    e.tensor_tensor(rk[:, :, :], R[:, 0:4, cc], R[:, 4:8, cc], ALU.mult).then_inc(po_c, 1)
                    mine("rk1")
                    e.tensor_tensor(rk[:, :, :], rk[:, :, :], r_k64[:, :].unsqueeze(2).broadcast_to([P, NP, C]),
                                    ALU.mult).then_inc(po_c, 1)

                chunk(0, True)
                with po.Fori(1, NCH) as i:
                    chunk(i, False)
                    after(i - 1, bass.ds((i - 1) * C, C))
                after(NCH - 1, bass.ds((NCH - 1) * C, C))
                with po.Fori(1, KT // 2) as it:
                    for s in range(2):
                        split(s, turn(s, l, PAIRS["out"] + it), KT * P)
                with po.Fori(0, HALVES) as h:
                    with po.Fori(0, FT) as it:
                        for s in range(2):
                            split(s, turn(s, l, PAIRS["ffn"] + h * FFN_PAIRS + it), KT * P)
                    with po.Fori(0, KT // 2) as it:
                        for s in range(2):
                            split(s, turn(s, l, PAIRS["ffn"] + h * FFN_PAIRS + FT + it), FT * P)

        @block.tensor
        def _(pe):
            e = nc.tensor

            def both(out, lhsT, rhs, start, stop):
                e.matmul(acc(out)[:, 0], lhsT, rhs[:, 0:HT], start=start, stop=stop)
                return e.matmul(acc(out)[:, 1], lhsT, rhs[:, HT:TOK], start=start, stop=stop)

            def turned(out, src, one, h):
                if h.start == 0:
                    return e.transpose(out, src, one)
                return e.matmul(out, src, one, start=True, stop=True)

            def passes(s, hi, lo, kt, kts):
                wh = whi[s][:, kt * P:(kt + 1) * P]
                wl = wlo[s][:, kt * P:(kt + 1) * P]
                for lhsT, rhs, a, z in ((wh, hi[:, kt], kt == 0, False), (wh, lo[:, kt], False, False),
                                        (wl, hi[:, kt], False, kt == kts - 1)):
                    mm = both(PS[s], lhsT, rhs, a, z)
                return mm

            def first_pair(l, pair, after_lowrank, ready, count):
                for s in range(2):
                    k = turn(s, l, pair, after_lowrank)
                    pe.wait_ge(w_lo[s], k + 1)
                    pe.wait_ge(psum_free[s], k)
                for kt in range(KT):
                    pe.wait_ge(ready, count + kt + 1)
                    for s in range(2):
                        mm = passes(s, xh, xl, kt, KT)
                        if kt == KT - 1:
                            mm.then_inc(tile_done[s], 1)

            def dense(s, k, hi, lo, kts):
                pe.wait_ge(w_lo[s], k + 1)
                pe.wait_ge(psum_free[s], k)
                for kt in range(kts):
                    mm = passes(s, hi, lo, kt, kts)
                mm.then_inc(tile_done[s], 1)

            pe.wait_ge(consts, N_CONSTS)
            for b, (t0, w) in enumerate(BLOCKS):
                pe.wait_ge(x_loaded, 32)
                if b >= 2:
                    pe.wait_ge(x_copied, b - 1)
                for k in range(KT):
                    mm = e.transpose(PS[b % 2][:, k * P:k * P + w], xin[0:w, b, k * P:(k + 1) * P], ident[0:w, 0:w])
                mm.then_inc(x_turned, 1)

            def norm_sum(c):
                pe.wait_ge(n_acc, (c + 1) * (KT + 1))
                both(nsum, mean128[:, :], nacc, True, True).then_inc(n_sum, 1)

            with pe.Fori(0, DEPTH) as l:
                pe.wait_ge(rows_loaded, (l + 1) * 16 * N_ROWS)
                pe.wait_ge(x_copied, len(BLOCKS))
                e.transpose(PS[3][:, 0:NA], rows_a[:, :], ident[0:NA, 0:NA])
                e.transpose(PS[3][:, NA:NA + NB], rows_b[:, :], ident[0:NB, 0:NB]).then_inc(par_turned, 1)
                norm_sum(l * NORMS)

                first_pair(l, PAIRS["rwkv"], False, n_lo, l * NORMS * KT)
                with pe.Fori(1, RT // 2) as it:
                    for s in range(2):
                        dense(s, turn(s, l, PAIRS["rwkv"] + it, False), xh, xl, KT)

                pe.wait_ge(small_loaded, (l + 1) * 64)
                for s in range(2):
                    pe.wait_ge(psum_free[s], turn(s, l, PAIRS["gla"], False))
                pe.wait_ge(pre_act, l * N_PRE_ACT + A_TANH)
                pe.wait_ge(par_ready, l * 3 + 3)
                for p in range(NP):
                    w = w2a2[0:64, p * P:(p + 1) * P]
                    v = R[0:64, 12]
                    e.matmul(PS[p][:, 0:512], w, v[:, 0:512], start=True, stop=True)
                    e.matmul(PS[p][:, 512:TOK], w, v[:, 512:TOK], start=True, stop=True).then_inc(pre_pe, 1)
                for p in range(NP):
                    pe.wait_ge(pre_act, l * N_PRE_ACT + A_W + p)
                    w = w2a2[64:128, p * P:(p + 1) * P]
                    v = R[64:128, 12]
                    e.matmul(PS[p][:, 0:512], w, v[:, 0:512], start=True, stop=True)
                    e.matmul(PS[p][:, 512:TOK], w, v[:, 512:TOK], start=True, stop=True).then_inc(pre_pe, 1)
                for p in range(NP):
                    pe.wait_ge(pre_act, l * N_PRE_ACT + A_A + p)
                    pe.wait_ge(pre_act, l * N_PRE_ACT + A_SQ + p)
                    both(PS[p], mean64[:, :], T[p], True, True).then_inc(pre_pe, 1)

                pe.wait_ge(pre_dve, l * N_PRE_DVE + D_MAX + 1)
                dense(0, turn(0, l, PAIRS["gla"], False), xh, xl, KT)
                pe.wait_ge(psum_free[0], turn(0, l, PAIRS["gla"], False) + 1)
                pe.wait_ge(pre_dve, l * N_PRE_DVE + D_MAX + 3)
                for q in range(2):
                    w = gw2[LR_AT:P, q * P:(q + 1) * P]
                    v = R[LR_AT:P, 12]
                    e.matmul(PS[2 + q][:, 0:512], w, v[:, 0:512], start=True, stop=True)
                    e.matmul(PS[2 + q][:, 512:TOK], w, v[:, 512:TOK], start=True, stop=True).then_inc(pre_pe, 1)
                with pe.Fori(0, GT // 2) as it:
                    for s in range(2):
                        dense(s, turn(s, l, PAIRS["gla"] + it), xh, xl, KT)

                def turn_state(src):
                    for p in range(NP):
                        for hp in range(2):
                            h = slice(64 * hp, 64 * hp + 64)
                            mm = turned(stat[h, p * C:(p + 1) * C], src[h, p, :], ident2[h, :], h)
                    mm.then_inc(st_pe, 1)

                pe.wait_ge(states_loaded, (l + 1) * 64)
                for s in range(2):
                    pe.wait_ge(psum_free[s], turn(s, l, PAIRS["out"]))
                pe.wait_ge(pre_dve, (l + 1) * N_PRE_DVE)
                apart(pe)
                turn_state(Sraw)
                pe.wait_ge(st_dve, l * 3 + 1)

                def after_a(i):
                    m = l * NCH + i
                    pe.wait_ge(ac_c, m * len(AC_C) + AC_C.index("YB") + 1)
                    pe.wait_ge(dv_c, m * len(DV_C) + DV_C.index("gate") + 1)
                    e.matmul(stat[:, 0:NP * C], mean64[:, :], Ych[:, :, :].rearrange("p a b -> p (a b)"),
                             start=True, stop=True).then_inc(pe_p, 1)
                    pe.wait_ge(ac_p, m * len(AC_P) + AC_P.index("osq") + 1)
                    e.matmul(oE[:, NP * C:2 * NP * C], mean128[:, :], SQ[:, NP * C:2 * NP * C],
                             start=True, stop=True).then_inc(pe_p, 1)

                def after_b(i):
                    m = l * NCH + i
                    pe.wait_ge(ac_p, m * len(AC_P) + AC_P.index("ysq") + 1)
                    e.matmul(oE[:, 0:NP * C], mean64[:, :], SQ[:, 0:NP * C], start=True, stop=True)\
                     .then_inc(pe_p, 1)

                def chunk(i, first):
                    n = l * NCH + i

                    def act(name, m=n):
                        pe.wait_ge(ac_c, m * len(AC_C) + AC_C.index(name) + 1)
                        apart(pe)

                    def dve(name, m=n):
                        pe.wait_ge(dv_c, m * len(DV_C) + DV_C.index(name) + 1)
                        apart(pe)

                    def pool(name, m=n):
                        pe.wait_ge(po_c, m * len(PO_C) + PO_C.index(name) + 1)
                        apart(pe)

                    def heads(X):
                        for q in range(2):
                            for hp in range(2):
                                yield 2 * X + q, slice(64 * hp, 64 * hp + 64), q

                    if not first:
                        after_a(i - 1)
                    dve("ke")
                    for q in range(2):
                        for hp in range(2):
                            h = slice(64 * hp, 64 * hp + 64)
                            mm = e.matmul(gm[h, q * C:(q + 1) * C], ke[h, q, :], qe[h, q, h], start=True, stop=True)
                    mm.then_inc(pe_c, 1)
                    pool("kd")
                    for q in range(2):
                        for hp in range(2):
                            h = slice(64 * hp, 64 * hp + 64)
                            turned(oO[h, q * GDV:(q + 1) * GDV], Vgs[:, 2 * q + hp, :], ident[:, :], h)
                            mm = turned(oO[h, 2 * GDV + q * C:2 * GDV + (q + 1) * C], kd[h, q, :], ident2[h, :], h)
                    mm.then_inc(pe_c, 1)
                    if not first:
                        after_b(i - 1)
                    dve("kt1")
                    pool("rt")
                    for X in range(2):
                        for q in range(2):
                            p = 2 * X + q
                            e.matmul(pq[X][:, q * P:(q + 1) * P], Bt[:, p, :], AR[:, p, :], start=True, stop=True)
                            e.matmul(pq[X][:, 256 + q * P:256 + (q + 1) * P], Kt[:, p, :], AR[:, p, :],
                                     start=True, stop=True)
                        for p, h, q in heads(X):
                            mm = e.matmul(tt[X][h, q * C:(q + 1) * C], AR[h, p, 0:C], Bt[h, p, h],
                                          start=True, stop=True)
                        mm.then_inc(pe_c, 1)
                    dve("g_scores1")
                    act("g_tok")
                    if not first:
                        pe.wait_ge(ac_p, (n - 1) * len(AC_P) + AC_P.index("oln") + 1)
                    for q in range(2):
                        o = oE[:, q * P:(q + 1) * P]
                        e.matmul(o, gtok[:, q * GDV:(q + 1) * GDV], scm[:, q, :], start=True, stop=False)
                        mm = e.matmul(o, Sg[:, q, :], qe[:, q, :], start=False, stop=True)
                    mm.then_inc(pe_c, 1)
                    for q in range(2):
                        for hp in range(2):
                            h = slice(64 * hp, 64 * hp + 64)
                            mm = e.matmul(gm[h, q * GDV:(q + 1) * GDV],
                                          gtok[h, 2 * GDV + q * C:2 * GDV + (q + 1) * C],
                                          gtok[h, q * GDV:(q + 1) * GDV], start=True, stop=True)
                    mm.then_inc(pe_c, 1)
                    pool("kh1")
                    for X, N in ((0, "A"), (1, "B")):
                        dve("X" + N)
                        for a, src in enumerate((Bh, Kh, Vs)):
                            for p, h, q in heads(X):
                                mm = turned(pq[X][h, (2 * a + q) * C:(2 * a + q + 1) * C], src[h, p, :],
                                            ident2[h, :], h)
                        mm.then_inc(pe_c, 1)
                    def square(out, X, src, both_ways=True):
                        for q in range(2):
                            mm = e.matmul(out[:, q * P:(q + 1) * P], src[:, X, 1, q], src[:, X, 0, q],
                                          start=True, stop=True)
                            if both_ways:
                                mm = e.matmul(out[:, (2 + q) * P:(3 + q) * P], src[:, X, 0, q], src[:, X, 1, q],
                                              start=True, stop=True)
                        mm.then_inc(pe_c, 1)

                    for X, N in ((0, "A"), (1, "B")):
                        dve("E" + N)
                        square(tt[X], X, DE[0])
                    for k in (2, 4, 8):
                        src = DE[1] if k != 4 else DE[0]
                        for X, N in ((0, "A"), (1, "B")):
                            if k == 2:
                                act("tok" + N)
                            act(f"D{k}{N}")
                            square(pq[X], X, src, k != 8)
                            dve(f"T{k // 2}{N}" if k > 2 else "T" + N)
                            for q in range(2):
                                mm = e.matmul(tt[X][:, q * P:(q + 1) * P], src[:, X, 0, q], Tt[:, X, q],
                                              start=True, stop=True)
                            mm.then_inc(pe_c, 1)
                    for X, N in ((0, "A"), (1, "B")):
                        act("D16" + N)
                        dve("T8" + N)
                        for q in range(2):
                            mm = e.matmul(tt[X][:, q * P:(q + 1) * P], DE[0][:, X, 0, q], Tt[:, X, q],
                                          start=True, stop=True)
                        mm.then_inc(pe_c, 1)
                    if not first:
                        dve("StB", n - 1)
                        pe.wait_ge(st_dve, l * 3 + 3)
                        apart(pe)
                    for X, N in ((0, "A"), (1, "B")):
                        for p, h, q in heads(X):
                            e.matmul(pq[X][h, q * C:(q + 1) * C], AR[h, p, 0:C], St[h, p, :], start=True, stop=False)
                            mm = e.matmul(pq[X][h, q * C:(q + 1) * C], KM[h, p, 0:C], tok[h, X, 2, q, :],
                                          start=False, stop=True)
                        mm.then_inc(pe_c, 1)
                    def solve(X, out, src):
                        for p, h, q in heads(X):
                            mm = e.matmul(out[h, q * C:(q + 1) * C], Tt[h, X, q, h.start:h.stop], src[h, p, :],
                                          start=True, stop=True)
                        mm.then_inc(pe_c, 1)

                    for X, N in ((0, "A"), (1, "B")):
                        act("Z" + N)
                        dve("T16" + N)
                        solve(X, tt[X], Z)
                    for X, N in ((0, "A"), (1, "B")):
                        act("Z1" + N)
                        for p, h, q in heads(X):
                            mm = e.matmul(pq[X][h, q * C:(q + 1) * C], Et[h, p, :], Z1[h, p, :],
                                          start=True, stop=True)
                        mm.then_inc(pe_c, 1)
                    for X, N in ((0, "A"), (1, "B")):
                        dve("Z2" + N)
                        solve(X, tt[X], W)
                    for X, N in ((0, "A"), (1, "B")):
                        act("U" + N)
                        for p, h, q in heads(X):
                            o = tt[X][h, q * C:(q + 1) * C]
                            e.matmul(o, St[h, p, :], AR[h, p, C:2 * C], start=True, stop=False)
                            e.matmul(o, U[h, p, :], QM[h, p, :], start=False, stop=False)
                            mm = e.matmul(o, tok[h, X, 2, q, :], KM[h, p, C:2 * C], start=False, stop=True)
                        mm.then_inc(pe_c, 1)
                        for p, h, q in heads(X):
                            o = pq[X][h, q * C:(q + 1) * C]
                            e.matmul(o, tok[h, X, 0, q, :], U[h, p, :], start=True, stop=False)
                            mm = e.matmul(o, tok[h, X, 1, q, :], tok[h, X, 2, q, :], start=False, stop=True)
                        mm.then_inc(pe_c, 1)
                    pool("rk")
                    if not first:
                        pe.wait_ge(dv_p, (n - 1) * len(DV_P) + DV_P.index("yc") + 1)
                    e.matmul(stat[:, 0:NP * C], mean64[:, :], rk[:, :, :].rearrange("p a b -> p (a b)"),
                             start=True, stop=True)
                    for p in range(NP):
                        mm = e.matmul(stat[:, (NP + p) * C:(NP + p + 1) * C], g2[:, p * P:(p + 1) * P],
                                      R[:, 13, bass.ds(i * C, C)], start=True, stop=True)
                    mm.then_inc(pe_c, 1)

                chunk(0, True)
                pe.wait_ge(dv_c, (l * NCH) * len(DV_C) + len(DV_C))
                apart(pe)
                turn_state(St)
                pe.wait_ge(kept, l * 4 + 2)
                apart(pe)
                with pe.Fori(1, NCH) as i:
                    chunk(i, False)
                after_a(NCH - 1)
                after_b(NCH - 1)
                pe.wait_ge(dv_p, (l * NCH + NCH - 1) * len(DV_P) + DV_P.index("yc") + 1)
                apart(pe)
                turn_state(St)

                first_pair(l, PAIRS["out"], True, m_lo, l * KT)
                with pe.Fori(1, KT // 2) as it:
                    for s in range(2):
                        dense(s, turn(s, l, PAIRS["out"] + it), xh, xl, KT)

                norm_sum(l * NORMS + 1)
                first_pair(l, PAIRS["ffn"], True, n_lo, (l * NORMS + 1) * KT)
                for h in range(HALVES):
                    with pe.Fori(1 if h == 0 else 0, FT) as it:
                        for s in range(2):
                            dense(s, turn(s, l, PAIRS["ffn"] + h * FFN_PAIRS + it), xh, xl, KT)
                    pe.wait_ge(f_dve, ((l * HALVES + h) * FT + FT) * F_STEPS)
                    apart(pe)
                    with pe.Fori(0, KT // 2) as it:
                        for s in range(2):
                            dense(s, turn(s, l, PAIRS["ffn"] + h * FFN_PAIRS + FT + it), hh, hl, FT)

                e.transpose(PS[3][0:2 * RT, 0:P], last_rows[:, :, :].rearrange("p a b -> p (a b)"), ident[:, :])
                e.transpose(PS[3][0:4 * (F // P), P:2 * P], last_conv[:, :, :].rearrange("p a b -> p (a b)"), ident[:, :])\
                 .then_inc(rows_turned, 1)
                pe.wait_ge(rows_copied, 2 * l + 2)

            norm_sum(DEPTH * NORMS)
            pe.wait_ge(n_t, (DEPTH * NORMS + 1) * KT)
            for b, (t0, w) in enumerate(BLOCKS):
                if b >= 2:
                    pe.wait_ge(y_copied, b - 1)
                for k in range(KT):
                    mm = e.transpose(PS[b % 2][0:w, k * P:(k + 1) * P], x[:, k, t0:t0 + w], ident[:, :])
                mm.then_inc(y_turned, 1)

        @block.scalar
        def _(ac):
            e = nc.scalar

            def norm(c):
                ac.wait_ge(n_sum, c + 1)
                e.activation(by_half(nln[:, :]), acc(nsum), ACT.Ln, scale=1.0 / KT, bias=scal[:, 0:1])\
                 .then_inc(n_rs, 1)
                ac.wait_ge(n_rs, 2 * c + 1)
                e.activation(nrs[:, :], nln[:, :], ACT.Exp, scale=-0.5).then_inc(n_rs, 1)

            def split(s, k, width=KT * P):
                ac.wait_ge(w_loaded[s], 16 * k + 16)
                e.activation(whi[s][:, 0:width], raw[s][:, 0:width], ACT.Copy).then_inc(w_hi[s], 1)

            def tile(s, k, width=KT * P):
                ac.wait_ge(tile_done[s], k + 1)
                if width:
                    split(s, k + 1, width)

            def norm_hi(c):
                for k in range(KT):
                    ac.wait_ge(n_t, c * KT + k + 1)
                    e.activation(xh[:, k, :], nt[k % 2][:, :], ACT.Copy).then_inc(n_hi, 1)

            ac.wait_ge(x_copied, len(BLOCKS))
            for k in range(KT):
                if k >= 2:
                    ac.wait_ge(n_acc, k)
                e.activation(nsq[k % 2], x[:, k, :], ACT.Square).then_inc(n_sq, 1)
            ac.wait_ge(consts, N_CONSTS)

            def added(l, pair, c, width, after):
                def step_(it, next_width):
                    for s in range(2):
                        tile(s, turn(s, l, pair + it), next_width)
                        if c is None:
                            continue
                        ac.wait_ge(psum_free[s], turn(s, l, pair + it) + 1)
                        ac.wait_ge(n_acc, c * (KT + 1) + 2 * it + s)
                        e.activation(nsq[s], x[:, bass.ds(2 * it + s, 1), :].squeeze(1), ACT.Square).then_inc(n_sq, 1)

                last = KT // 2 - 1
                with ac.Fori(0, last) as it:
                    step_(it, width)
                step_(last, after)

            with ac.Fori(0, DEPTH) as l:
                for s in range(2):
                    ac.wait_ge(tile_done[s], turn(s, l, 0, False))
                    split(s, turn(s, l, 0, False))
                norm(l * NORMS)
                norm_hi(l * NORMS)
                with ac.Fori(0, RT // 2) as it:
                    for s in range(2):
                        tile(s, turn(s, l, PAIRS["rwkv"] + it, False))
                        ac.wait_ge(psum_free[s], turn(s, l, PAIRS["rwkv"] + it, False))
                        e.activation(by_half(T[s][:, 1:1 + TOK]), acc(PS[s]), ACT.Copy).then_inc(r_prev, 1)
                for s in range(2):
                    ac.wait_ge(psum_free[s], turn(s, l, PAIRS["gla"], False))
                b = l * N_PRE_ACT
                e.activation(R[0:64, 12, :], R[0:64, 12, :], ACT.Tanh).then_inc(pre_act, 1)
                e.activation(R[:, 13, :], R[:, 13, :], ACT.Sigmoid).then_inc(pre_act, 1)
                ac.wait_ge(pre_dve, l * N_PRE_DVE + D_ZERO)
                for p in range(NP):
                    ac.wait_ge(pre_pe, l * N_PRE_PE + p + 1)
                    o = cum[:, p, :].rearrange("p (c t) -> p c t", t=CP)[:, :, 1:CP]
                    e.activation(o, PS[p][:, 0:TOK].rearrange("p (c t) -> p c t", t=C), ACT.Sigmoid,
                                 bias=pcol("w0", p)).then_inc(pre_act, 1)
                for p in range(NP):
                    ac.wait_ge(pre_pe, l * N_PRE_PE + NP + p + 1)
                    e.activation(KA[:, p, :], PS[p][:, 0:TOK], ACT.Sigmoid, bias=pcol("a0", p)).then_inc(pre_act, 1)
                for p in range(NP):
                    ac.wait_ge(pre_dve, l * N_PRE_DVE + D_KK + p)
                    e.activation(T[p][:, 0:TOK], KK[:, p, :], ACT.Square).then_inc(pre_act, 1)
                for p in range(NP):
                    ac.wait_ge(pre_dve, l * N_PRE_DVE + D_MAX + p)
                    e.activation(T[p][:, 0:TOK], T[p][:, 0:TOK], ACT.Ln, scale=float(2 ** 26)).then_inc(pre_act, 1)
                    ac.wait_ge(pre_act, b + A_LN + 2 * p)
                    e.activation(T[p][:, 0:TOK], T[p][:, 0:TOK], ACT.Exp, scale=-0.5, bias=scal[:, 1:2])\
                     .then_inc(pre_act, 1)
                tile(0, turn(0, l, PAIRS["gla"], False))
                e.activation(by_half(R[LR_AT:P, 12, :]), acc(PS[0])[LR_AT:P], ACT.Copy).then_inc(psum_free[0], 1)
                for q in range(2):
                    ac.wait_ge(pre_dve, l * N_PRE_DVE + D_ABS + 2 * q)
                    e.activation(T[2 * q + 1][:, 0:TOK], T[2 * q + 1][:, 0:TOK], ACT.Exp, scale=-1.0).then_inc(pre_act, 1)
                    ac.wait_ge(pre_act, b + A_GE + 2 * q)
                    e.activation(T[2 * q + 1][:, 0:TOK], T[2 * q + 1][:, 0:TOK], ACT.Ln, bias=1.0).then_inc(pre_act, 1)
                with ac.Fori(0, 4) as it:
                    for s in range(2):
                        tile(s, turn(s, l, PAIRS["gla"] + it))
                        e.activation(by_half(G[:, bass.ds(2 * it + s, 1), :].squeeze(1)), acc(PS[s]), ACT.Copy)\
                         .then_inc(psum_free[s], 1)
                with ac.Fori(4, 6) as it:
                    for s in range(2):
                        tile(s, turn(s, l, PAIRS["gla"] + it))
                        e.activation(by_half(G[:, bass.ds(2 * it + s, 1), :].squeeze(1)), acc(PS[s]), ACT.Silu)\
                         .then_inc(psum_free[s], 1)
                ac.wait_ge(psum_free[0], turn(0, l, PAIRS["out"]))
                ac.wait_ge(psum_free[1], turn(1, l, PAIRS["out"]))
                ac.wait_ge(pre_dve, (l + 1) * N_PRE_DVE)

                def after_a(i):
                    m = l * NCH + i
                    ac.wait_ge(ac_c, m * len(AC_C) + AC_C.index("g_o") + 1)
                    e.activation(SQo, Och[:, :, :], ACT.Square).then_inc(ac_p, 1)
                    ac.wait_ge(dv_p, m * len(DV_P) + DV_P.index("yc") + 1)
                    e.activation(SQy, Yc, ACT.Square).then_inc(ac_p, 1)

                def after_b(i):
                    m = l * NCH + i
                    ac.wait_ge(pe_p, m * len(PE_P) + PE_P.index("yvar") + 1)
                    e.activation(SQ[:, 0:NP * C], oE[:, 0:NP * C], ACT.Ln, bias=scal[:, 2:3]).then_inc(ac_p, 1)
                    e.activation(SQ[:, NP * C:], oE[:, NP * C:2 * NP * C], ACT.Ln, bias=scal[:, 0:1]).then_inc(ac_p, 1)
                    ac.wait_ge(ac_p, m * len(AC_P) + AC_P.index("oln") + 1)
                    e.activation(SQ, SQ, ACT.Exp, scale=-0.5).then_inc(ac_p, 1)

                def chunk(i, first):
                    n = l * NCH + i
                    pc = bass.ds(i * CP, CP)

                    def pe(name):
                        ac.wait_ge(pe_c, n * len(PE_C) + PE_C.index(name) + 1)

                    def copy(out, in_):
                        e.activation(out, in_, ACT.Copy).then_inc(ac_c, 1)

                    if not first:
                        ac.wait_ge(po_c, n * len(PO_C))
                    e.activation(Pp[:, :, :], cum[:, :, pc], ACT.Exp, scale=-KAPPA).then_inc(ac_c, 1)
                    if not first:
                        ac.wait_ge(dv_c, (n - 1) * len(DV_C) + DV_C.index("kt1") + 1)
                    e.activation(Pinv[:, :, :], cum[:, :, bass.ds(i * CP + 1, C)], ACT.Exp, scale=KAPPA).then_inc(ac_c, 1)
                    if not first:
                        ac.wait_ge(dv_c, (n - 1) * len(DV_C) + DV_C.index("Sg1") + 1)
                    e.activation(Eg[:, :, :], cg[:, :, bass.ds(i * CP + 1, C)], ACT.Exp, scale=1.0 / 16).then_inc(ac_c, 1)
                    e.activation(Ei[:, :, :], cg[:, :, bass.ds(i * CP + 1, C)], ACT.Exp, scale=-1.0 / 16).then_inc(ac_c, 1)
                    if not first:
                        after_a(i - 1)
                    pe("g_tok")
                    copy(gtok[:, :], oO[:, 0:2 * GDV + 2 * C])
                    if not first:
                        after_b(i - 1)
                    pe("g_out")
                    if not first:
                        ac.wait_ge(dv_p, (n - 1) * len(DV_P) + DV_P.index("on") + 1)
                    copy(Och[:, :, :], pair3(oE[:, 0:GH * C]))
                    for X, N in ((0, "A"), (1, "B")):
                        pe("tok" + N)
                        copy(tok[:, X].rearrange("p a q t -> p (a q t)"), pq[X][:, 0:6 * C])
                    for k in (2, 4, 8, 16):
                        for X, N in ((0, "A"), (1, "B")):
                            pe(f"D{k}{N}")
                            both_ways = 2 if k != 16 else 1
                            dst = DE[1] if k in (2, 8) else DE[0]
                            if k == 4:
                                ac.wait_ge(dv_c, n * len(DV_C) + DV_C.index("T" + N) + 1)
                            elif k > 4:
                                pe(f"T{k // 4}{N}")
                            copy(dst[:, X, 0:both_ways].rearrange("p d q t -> p (d q t)"),
                                 (tt if k == 2 else pq)[X][:, 0:both_ways * 2 * P])

                    def own(t, X):
                        return t[:, 2 * X:2 * X + 2, :].rearrange("p q t -> p (q t)")

                    for X, N in ((0, "A"), (1, "B")):
                        pe("Z" + N)
                        copy(own(Z, X), pq[X][:, 0:2 * C])
                    for X, N in ((0, "A"), (1, "B")):
                        pe("Z1" + N)
                        copy(own(Z1, X), tt[X][:, 0:2 * C])
                    for X, N in ((0, "A"), (1, "B")):
                        pe("U" + N)
                        copy(own(U, X), tt[X][:, 0:2 * C])
                    for X, N in ((0, "A"), (1, "B")):
                        pe("Y" + N)
                        copy(Ych[:, 2 * X:2 * X + 2, :].rearrange("p q t -> p (q t)"), tt[X][:, 0:2 * C])

                def store_states(c, gla, rwkv):
                    ac.wait_ge(kept, l * 4 + c)
                    for hp in range(2):
                        h = slice(64 * hp, 64 * hp + 64)
                        ac.dma_start(gla[l, 0].rearrange("(q h) d v -> h d q v", h=2)[hp], SgO[h])\
                          .then_inc(states_out, 16)
                        ac.dma_start(rwkv[l, 0].rearrange("(q h) v k -> h v q k", h=2)[hp], StT[h])\
                          .then_inc(states_out, 16)

                chunk(0, True)
                store_states(2, gla_s, rwkv_s)
                with ac.Fori(1, NCH) as i:
                    chunk(i, False)
                after_a(NCH - 1)
                after_b(NCH - 1)

                ac.wait_ge(dv_p, (l + 1) * NCH * len(DV_P))
                ac.wait_ge(po_p, (l + 1) * NCH * len(PO_P))
                store_states(4, gla_p, rwkv_p)
                for k in range(KT):
                    src = G[:, 4 + k, :] if k < 4 else R[:, k - 4, :]
                    e.activation(xh[:, k, :], src, ACT.Copy).then_inc(m_hi, 1)

                added(l, PAIRS["out"], l * NORMS + 1, KT * P, KT * P)
                ac.wait_ge(states_out, (l + 1) * 128)
                norm(l * NORMS + 1)
                norm_hi(l * NORMS + 1)
                ac.wait_ge(n_lo, (l * NORMS + 2) * KT)
                ac.wait_ge(up_pad, l + 1)

                def widen_tile(h, it, next_width):
                    t = (l * HALVES + h) * FT + it
                    tile(0, turn(0, l, PAIRS["ffn"] + h * FFN_PAIRS + it), next_width)
                    ac.wait_ge(f_dve, t * F_STEPS)
                    e.activation(up[:, 2:2 + DEC], PS[0][:, 0:DEC], ACT.Copy)
                    e.activation(up[:, 4 + DEC:4 + HT], PS[0][:, DEC:HT], ACT.Copy)
                    e.activation(up[:, 4 + HT:4 + TOK], acc(PS[0])[:, 1], ACT.Copy).then_inc(psum_free[0], 1)
                    ac.wait_ge(f_dve, t * F_STEPS + 6)
                    e.activation(gl[:, :], cv[:, :], ACT.Gelu).then_inc(f_gelu, 1)
                    tile(1, turn(1, l, PAIRS["ffn"] + h * FFN_PAIRS + it), next_width)
                    ac.wait_ge(psum_free[1], turn(1, l, PAIRS["ffn"] + h * FFN_PAIRS + it) + 1)
                    e.activation(HH(it), hf[:, :], ACT.Copy).then_inc(f_hi, 1)

                def HH(it):
                    return hh[:, it, :] if isinstance(it, int) else hh[:, bass.ds(it, 1), :].squeeze(1)

                for h in range(HALVES):
                    last_half = h == HALVES - 1
                    with ac.Fori(0, FT - 1) as it:
                        widen_tile(h, it, KT * P)
                    widen_tile(h, FT - 1, FT * P)
                    added(l, PAIRS["ffn"] + h * FFN_PAIRS + FT, (l + 1) * NORMS if last_half else None,
                          FT * P, 0 if last_half else KT * P)
                ac.wait_ge(rows_turned, l + 1)
                ac.wait_ge(stored, l * 64)
                e.activation(rowout[0:2 * RT, 0, :], PS[3][0:2 * RT, 0:P], ACT.Copy).then_inc(rows_copied, 1)
                e.activation(rowout[0:4 * (F // P), 1, :], PS[3][0:4 * (F // P), P:2 * P], ACT.Copy)\
                 .then_inc(rows_copied, 1)
                ac.wait_ge(rows_copied, 2 * l + 2)
                for g, (sh, co) in enumerate(((shift_s, conv_s), (shift_p, conv_p))):
                    ac.dma_start(sh[l, 0].rearrange("(k p) -> k p", p=P), rowout[g * RT:(g + 1) * RT, 0, :])\
                      .then_inc(stored, 16)
                    n = 2 * (F // P)
                    ac.dma_start(co[l, 0].rearrange("r (k p) -> (r k) p", p=P), rowout[g * n:(g + 1) * n, 1, :])\
                      .then_inc(stored, 16)

            norm(DEPTH * NORMS)
            for b, (t0, w) in enumerate(BLOCKS):
                ac.wait_ge(y_turned, b + 1)
                if b >= 2:
                    ac.wait_ge(y_stored[b % 2], 16 * (b // 2))
                e.activation(yout[0:w, b % 2, :], PS[b % 2][0:w, :], ACT.Copy).then_inc(y_copied, 1)
                ac.wait_ge(y_copied, b + 1)
                dst = y_sample[0] if b == 0 else y_prompt[0, t0 - DEC:t0 - DEC + w, :]
                ac.dma_start(dst, yout[0:w, b % 2, :]).then_inc(y_stored[b % 2], 16)
            for i in range(2):
                ac.wait_ge(y_stored[i], 16 * ((len(BLOCKS) + 1 - i) // 2))
            ac.wait_ge(stored, 64 * DEPTH)
            ac.wait_ge(states_out, 128 * DEPTH)

        @block.vector
        def _(dv):
            e = nc.vector
            for b, (t0, w) in enumerate(BLOCKS):
                dv.wait_ge(x_turned, b + 1)
                e.tensor_copy(x[:, :, t0:t0 + w], PS[b % 2][:, :].rearrange("p (k t) -> p k t", t=P)[:, :, 0:w])\
                 .then_inc(x_copied, 1)
            dv.wait_ge(consts, N_CONSTS)

            def norm(c, name):
                dv.wait_ge(n_rs, 2 * c + 2)

                def normed(k):
                    if k >= 2:
                        dv.wait_ge(n_lo, c * KT + k - 1)
                    e.scalar_tensor_tensor(out=nt[k % 2][:, :], in0=x[:, k, :], scalar=pcol(name, k),
                                           in1=nrs[:, :], op0=ALU.mult, op1=ALU.mult).then_inc(n_t, 1)

                normed(0)
                for k in range(KT):
                    if k + 1 < KT:
                        normed(k + 1)
                    dv.wait_ge(n_hi, c * KT + k + 1)
                    e.tensor_tensor(xl[:, k, :], nt[k % 2][:, :], xh[:, k, :].bitcast(F32), ALU.subtract)\
                     .then_inc(n_lo, 1)

            def clear_squares():
                e.memset(nacc, 0.0).then_inc(n_acc, 1)

            def add_square(c, k, s):
                dv.wait_ge(n_sq, c * KT + k + 1)
                dv.wait_ge(n_acc, c * (KT + 1) + k + 1)
                e.tensor_tensor(nacc, nacc, nsq[s], ALU.add).then_inc(n_acc, 1)

            clear_squares()
            for k in range(KT):
                add_square(0, k, k % 2)

            with dv.Fori(0, DEPTH) as l:
                dv.wait_ge(par_turned, l + 1)
                e.tensor_copy(par[:, :], PS[3][:, 0:NA + NB]).then_inc(par_ready, 1)
                dv.wait_ge(par_ready, l * 3 + 1)
                e.tensor_scalar(one_ka[:, :], pcol("k_a", 0, NP), -1.0, 1.0, ALU.mult, ALU.add).then_inc(par_ready, 1)
                e.tensor_scalar(r_k64[:, :], pcol("r_k", 0, NP), 64.0, None, ALU.mult).then_inc(par_ready, 1)
                norm(l * NORMS, "norm_mix")

                mu, shift = ROWS_A["mu"][0], ROWS_A["shift"][0]
                with dv.Fori(0, RT // 2) as it:
                    for s in range(2):
                        j = 2 * it + s
                        t = (l * RT + j) * R_STEPS
                        dv.wait_ge(r_prev, l * RT + j + 1)
                        pv = T[s]
                        e.tensor_copy(last_rows[:, :, bass.ds(j, 1)], pv[:, 64:TOK + 1:SEQ].unsqueeze(2)).then_inc(r_dve, 1)
                        dv.wait_ge(r_dve, t + 1)
                        e.tensor_copy(pv[:, 0:1], par[:, bass.ds(shift + j, 1)]).then_inc(r_dve, 1)
                        e.memset(pv[:, 64:65], 0.0).then_inc(r_dve, 1)
                        dv.wait_ge(r_dve, t + 3)
                        e.tensor_tensor(by_half(T[2][:, 0:TOK]), by_half(pv[:, 0:TOK]), acc(PS[s]), ALU.subtract).then_inc(r_dve, 1)
                        dv.wait_ge(r_dve, t + 4)
                        e.scalar_tensor_tensor(out=by_half(R[:, bass.ds(j, 1), :].squeeze(1)), in0=by_half(T[2][:, 0:TOK]),
                                               scalar=par[:, bass.ds(mu + j, 1)], in1=acc(PS[s]),
                                               op0=ALU.mult, op1=ALU.add).then_inc(psum_free[s], 1)

                b = l * N_PRE_DVE
                done = 0

                def step(ins):
                    nonlocal done
                    done += 1
                    ins.then_inc(pre_dve, 1)

                def mine():
                    dv.wait_ge(pre_dve, b + done)

                step(e.memset(cum[:, :, :].rearrange("p a (c t) -> p a c t", t=CP)[:, :, :, 0], 0.0))
                step(e.memset(cg[:, :, :].rearrange("p a (c t) -> p a c t", t=CP)[:, :, :, 0], 0.0))
                assert done == D_ZERO
                for s in range(2):
                    dv.wait_ge(psum_free[s], turn(s, l, PAIRS["gla"], False))
                for p in range(NP):
                    step(e.tensor_scalar(KK[:, p, :], R[:, 4 + p, :], pcol("k_k", p), None, ALU.mult))
                    assert done == D_KK + p
                for p in range(NP):
                    dv.wait_ge(pre_act, l * N_PRE_ACT + A_W + p)
                    step(e.tensor_tensor_scan(cum[:, p, :], restart[:, :], cum[:, p, :], 0.0, ALU.mult, ALU.add))
                for p in range(NP):
                    dv.wait_ge(pre_pe, l * N_PRE_PE + 2 * NP + p + 1)
                    step(e.tensor_scalar(by_half(T[p][:, 0:TOK]), acc(PS[p]), 1e-24 / 64, None, ALU.max))
                    assert done == D_MAX + p
                for p in range(NP):
                    dv.wait_ge(pre_act, l * N_PRE_ACT + A_LN + 2 * p + 1)
                    step(e.tensor_tensor(KK[:, p, :], KK[:, p, :], T[p][:, 0:TOK], ALU.mult))
                    mine()
                    step(e.tensor_scalar(T[p][:, 0:TOK], KA[:, p, :], pcol("k_a", p), one_ka[:, p:p + 1], ALU.mult, ALU.add))
                    mine()
                    step(e.tensor_tensor(R[:, 4 + p, :], R[:, 4 + p, :], T[p][:, 0:TOK], ALU.mult))
                    step(e.tensor_tensor(KA[:, p, :], KK[:, p, :], KA[:, p, :], ALU.mult))
                    mine()
                for q in range(2):
                    dv.wait_ge(pre_pe, l * N_PRE_PE + 3 * NP + q + 1)
                    step(e.tensor_scalar(T[2 * q][:, 0:TOK], PS[2 + q][:, 0:TOK], pcol("gate_b", q), None, ALU.add))
                    mine()
                    step(e.scalar_tensor_tensor(out=T[2 * q + 1][:, 0:TOK], in0=T[2 * q][:, 0:TOK], scalar=-1.0,
                                                in1=T[2 * q][:, 0:TOK], op0=ALU.mult, op1=ALU.max))
                    assert done == D_ABS + 2 * q
                for q in range(2):
                    dv.wait_ge(pre_act, l * N_PRE_ACT + A_GE + 2 * q + 1)
                    v = cg[:, q, :].rearrange("p (c t) -> p c t", t=CP)
                    step(e.scalar_tensor_tensor(out=v[:, :, 1:CP], in0=pair3(T[2 * q][:, 0:TOK]), scalar=0.0,
                                                in1=pair3(T[2 * q + 1][:, 0:TOK]), op0=ALU.min, op1=ALU.subtract))
                    mine()
                    step(e.tensor_tensor_scan(cg[:, q, :], restart[:, :], cg[:, q, :], 0.0, ALU.mult, ALU.add))
                mine()
                assert done == N_PRE_DVE

                for s in range(2):
                    dv.wait_ge(psum_free[s], turn(s, l, PAIRS["out"]))
                for block_diagonal in (Bt, Kt, qe, scm):
                    e.memset(block_diagonal[:, :, :], 0.0).then_inc(cleared, 1)
                dv.wait_ge(cleared, (l + 1) * 4)
                dv.wait_ge(st_pe, l * 3 + 1)
                e.tensor_copy(St[:, :, :], pair3(stat[:, 0:NP * C])).then_inc(st_dve, 1)
                dv.wait_ge(states_loaded, (l + 1) * 64)

                def after_a(i):
                    m = l * NCH + i
                    dv.wait_ge(pe_p, m * len(PE_P) + PE_P.index("ymean") + 1)
                    e.scalar_tensor_tensor(out=Yc, in0=pair3(stat[:, 0:NP * C]), scalar=-1.0, in1=Ych[:, :, :],
                                           op0=ALU.mult, op1=ALU.add).then_inc(dv_p, 1)

                def after_b(i):
                    m = l * NCH + i
                    dv.wait_ge(ac_p, m * len(AC_P) + AC_P.index("rstd") + 1)
                    dv.wait_ge(po_p, m * len(PO_P))
                    e.tensor_tensor(Yc, Yc, SQy, ALU.mult).then_inc(dv_p, 1)
                    e.scalar_tensor_tensor(out=On, in0=Och[:, :, :], scalar=pcol("gla_w"), in1=SQo,
                                           op0=ALU.mult, op1=ALU.mult).then_inc(dv_p, 1)

                def after_c(i, cc):
                    m = l * NCH + i
                    dv.wait_ge(po_p, m * len(PO_P) + PO_P.index("yb") + 1)
                    e.tensor_tensor(Yc, Yc, BV, ALU.add).then_inc(dv_p, 1)
                    dv.wait_ge(dv_p, m * len(DV_P) + DV_P.index("ybonus") + 1)
                    e.tensor_tensor(R[:, 0:4, cc], Yc, Gt, ALU.mult).then_inc(dv_p, 1)

                def chunk(i, first):
                    n = l * NCH + i
                    cc = bass.ds(i * C, C)

                    def pe(name):
                        dv.wait_ge(pe_c, n * len(PE_C) + PE_C.index(name) + 1)

                    def act(name):
                        dv.wait_ge(ac_c, n * len(AC_C) + AC_C.index(name) + 1)

                    def mine(name):
                        dv.wait_ge(dv_c, n * len(DV_C) + DV_C.index(name) + 1)

                    def before(sem_, order, name):
                        if not first:
                            dv.wait_ge(sem_, (n - 1) * len(order) + order.index(name) + 1)

                    if not first:
                        after_a(i - 1)
                    act("Ei")
                    halves = (slice(0, C), slice(C, 2 * C))
                    for h in halves:
                        e.scalar_tensor_tensor(out=qe[h, :, h], in0=G[h, 0:2, cc], scalar=0.125, in1=Eg[h, :, :],
                                               op0=ALU.mult, op1=ALU.mult).then_inc(dv_c, 1)
                    before(po_c, PO_C, "kd")
                    e.tensor_tensor(ke[:, :, :], G[:, 2:4, cc], Ei[:, :, :], ALU.mult).then_inc(dv_c, 1)
                    before(pe_c, PE_C, "YB")
                    e.scalar_tensor_tensor(out=AR[:, :, 0:C], in0=KK[:, :, cc], scalar=-1.0, in1=Pp[:, :, 0:C],
                                           op0=ALU.mult, op1=ALU.mult).then_inc(dv_c, 1)
                    before(po_c, PO_C, "kh1")
                    for dst, src in ((Bt, KA), (Kt, R[:, 4:8])):
                        for h in halves:
                            e.tensor_tensor(dst[h, :, h], src[h, :, cc], Pinv[h, :, :], ALU.mult).then_inc(dv_c, 1)
                    pe("g_scores")
                    for h in halves:
                        e.tensor_tensor(scm[h, :, h], pair3(gm[h, 0:2 * C]),
                                        m_si[h, C:2 * C].unsqueeze(1).broadcast_to([C, 2, C]), ALU.mult)\
                         .then_inc(dv_c, 1)
                    if not first:
                        after_b(i - 1)
                    for X, N in ((0, "A"), (1, "B")):
                        pp = slice(2 * X, 2 * X + 2)
                        pe("gram" + N)
                        four = [P, 2, 2, C]
                        gB, gK = pair3(pq[X][:, 0:256], P), pair3(pq[X][:, 256:512], P)
                        for src, m, d in ((pair3(tt[X][:, 0:2 * C]), m_bd, 0), (gB[:, :, 0:C], m_be, 1)):
                            e.tensor_tensor(DE[0][:, X, d].rearrange("p q (h t) -> p q h t", t=C),
                                            src.unsqueeze(2).broadcast_to(four),
                                            pair3(m[:, :]).unsqueeze(1).broadcast_to(four), ALU.mult).then_inc(dv_c, 1)
                        mine("E" + N)
                        e.tensor_tensor(Tt[:, X], DE[0][:, X, 1], ident[:, :].unsqueeze(1).broadcast_to([P, 2, P]),
                                        ALU.add).then_inc(dv_c, 1)
                        e.tensor_tensor(QM[:, pp, :], gB[:, :, C:2 * C],
                                        m_si[:, C:2 * C].unsqueeze(1).broadcast_to([P, 2, C]), ALU.mult).then_inc(dv_c, 1)
                        e.tensor_tensor(KM[:, pp, :], gK,
                                        m_si[:, :].unsqueeze(1).broadcast_to([P, 2, P]), ALU.mult).then_inc(dv_c, 1)
                        e.tensor_tensor(Et[:, pp, :], gB[:, :, 0:C],
                                        m_et[:, :].unsqueeze(1).broadcast_to([P, 2, C]), ALU.mult).then_inc(dv_c, 1)
                    if not first:
                        after_c(i - 1, bass.ds((i - 1) * C, C))
                    pe("g_state")
                    for q in range(2):
                        e.scalar_tensor_tensor(out=Sg[:, q, :], in0=Sg[:, q, :], scalar=Eg[:, q, C - 1:C],
                                               in1=gm[:, q * GDV:(q + 1) * GDV], op0=ALU.mult, op1=ALU.add)\
                         .then_inc(dv_c, 1)
                    for k in (2, 4, 8, 16):
                        for X, N in ((0, "A"), (1, "B")):
                            pe(f"T{k}{N}")
                            mine("T" + N if k == 2 else f"T{k // 2}{N}")
                            e.tensor_tensor(Tt[:, X], Tt[:, X], pair3(tt[X][:, 0:2 * P], P), ALU.add).then_inc(dv_c, 1)
                    for X, N in ((0, "A"), (1, "B")):
                        pe("Z2" + N)
                        pp = slice(2 * X, 2 * X + 2)
                        e.tensor_tensor(W[:, pp, :], Z[:, pp, :], pair3(pq[X][:, 0:2 * C]), ALU.add).then_inc(dv_c, 1)
                    dv.wait_ge(po_c, n * len(PO_C) + PO_C.index("stp") + 1)
                    for X, N in ((0, "A"), (1, "B")):
                        pp = slice(2 * X, 2 * X + 2)
                        pe("S" + N)
                        e.tensor_tensor(St[:, pp, :], StP[:, pp, :], pair3(pq[X][:, 0:2 * C]), ALU.add)\
                         .then_inc(dv_c, 1)
                    pe("bonus")
                    e.tensor_tensor(BV, pair3(stat[:, 0:NP * C]), R[:, 8:12, cc], ALU.mult).then_inc(dv_c, 1)
                    e.tensor_copy(Gt, pair3(stat[:, NP * C:2 * NP * C])).then_inc(dv_c, 1)

                def keep_states(c, i):
                    dv.wait_ge(st_pe, l * 3 + c)
                    dv.wait_ge(dv_c, (l * NCH + i + 1) * len(DV_C))
                    e.tensor_copy(SgO, Sg[:, :, :]).then_inc(kept, 1)
                    e.tensor_copy(StT, pair3(stat[:, 0:NP * C])).then_inc(kept, 1)

                chunk(0, True)
                keep_states(2, 0)
                dv.wait_ge(kept, l * 4 + 2)
                dv.wait_ge(pe_c, (l * NCH + 1) * len(PE_C))
                e.memset(Sg[:, :, :], 0.0).then_inc(st_dve, 1)
                e.memset(St[:, :, :], 0.0).then_inc(st_dve, 1)
                with dv.Fori(1, NCH) as i:
                    chunk(i, False)
                after_a(NCH - 1)
                after_b(NCH - 1)
                after_c(NCH - 1, bass.ds((NCH - 1) * C, C))
                dv.wait_ge(states_out, l * 128 + 64)
                keep_states(3, NCH - 1)

                for k in range(KT):
                    src = G[:, 4 + k, :] if k < 4 else R[:, k - 4, :]
                    dv.wait_ge(m_hi, l * KT + k + 1)
                    e.tensor_tensor(xl[:, k, :], src, xh[:, k, :].bitcast(F32), ALU.subtract).then_inc(m_lo, 1)
                dv.wait_ge(states_out, (l + 1) * 128)
                apart(dv)

                def add_tiles(pair, c=None):
                    if c is not None:
                        clear_squares()
                    with dv.Fori(0, KT // 2) as it:
                        for s in range(2):
                            xt = x[:, bass.ds(2 * it + s, 1), :].squeeze(1)
                            dv.wait_ge(tile_done[s], turn(s, l, pair + it) + 1)
                            e.tensor_tensor(by_half(xt), by_half(xt), acc(PS[s]), ALU.add).then_inc(psum_free[s], 1)
                            if c is not None:
                                add_square(c, 2 * it + s, s)

                add_tiles(PAIRS["out"], l * NORMS + 1)
                norm(l * NORMS + 1, "norm_ffn")

                e.memset(up[:, 2 + DEC:4 + DEC], 0.0).then_inc(up_pad, 1)
                cw, cb, cache = NA + ROWS_B["conv_w"][0], NA + ROWS_B["conv_b"][0], ROWS_A["cache"][0]
                FF = F // P

                def widen(h):
                    with dv.Fori(0, FT) as it:
                        t = (l * HALVES + h) * FT + it
                        f = h * FT + it
                        q = t * F_STEPS

                        def mine(c):
                            dv.wait_ge(f_dve, q + c)

                        mine(0)
                        e.tensor_copy(up[:, 0:2].unsqueeze(2),
                                      par[:, cache:cache + 2 * FF].rearrange("p (r k) -> p r k", r=2)[:, :, bass.ds(f, 1)])\
                         .then_inc(f_dve, 1)
                        dv.wait_ge(psum_free[0], turn(0, l, PAIRS["ffn"] + h * FFN_PAIRS + it) + 1)
                        mine(1)
                        e.tensor_scalar(cv[:, :], up[:, 0:2 + TOK], par[:, bass.ds(cw + f, 1)], par[:, bass.ds(cb + f, 1)],
                                        ALU.mult, ALU.add).then_inc(f_dve, 1)
                        for r in range(2):
                            e.tensor_copy(last_conv[:, r:4:2, bass.ds(f, 1)],
                                          up[:, 64 + r:580:SEQ + 2].unsqueeze(2)).then_inc(f_dve, 1)
                        mine(2)
                        e.scalar_tensor_tensor(out=cv[:, :], in0=up[:, 1:3 + TOK], scalar=par[:, bass.ds(cw + FF + f, 1)],
                                               in1=cv[:, :], op0=ALU.mult, op1=ALU.add).then_inc(f_dve, 1)
                        mine(5)
                        e.scalar_tensor_tensor(out=cv[:, :], in0=up[:, 2:4 + TOK], scalar=par[:, bass.ds(cw + 2 * FF + f, 1)],
                                               in1=cv[:, :], op0=ALU.mult, op1=ALU.add).then_inc(f_dve, 1)
                        dv.wait_ge(tile_done[1], turn(1, l, PAIRS["ffn"] + h * FFN_PAIRS + it) + 1)
                        dv.wait_ge(f_gelu, t + 1)
                        e.tensor_tensor(hf[:, 0:DEC], gl[:, 0:DEC], PS[1][:, 0:DEC], ALU.mult).then_inc(f_dve, 1)
                        e.tensor_tensor(hf[:, DEC:HT], gl[:, DEC + 2:HT + 2], PS[1][:, DEC:HT], ALU.mult).then_inc(f_dve, 1)
                        e.tensor_tensor(hf[:, HT:TOK], gl[:, HT + 2:TOK + 2], acc(PS[1])[:, 1], ALU.mult)\
                         .then_inc(psum_free[1], 1)
                        dv.wait_ge(f_hi, t + 1)
                        e.tensor_tensor(hl[:, bass.ds(it, 1), :].squeeze(1), hf[:, :],
                                        hh[:, bass.ds(it, 1), :].squeeze(1).bitcast(F32), ALU.subtract)\
                         .then_inc(f_dve, 1)

                for h in range(HALVES):
                    widen(h)
                    add_tiles(PAIRS["ffn"] + h * FFN_PAIRS + FT, (l + 1) * NORMS if h == HALVES - 1 else None)

            c = DEPTH * NORMS
            dv.wait_ge(n_rs, 2 * c + 2)
            for k in range(KT):
                e.scalar_tensor_tensor(out=x[:, k, :], in0=x[:, k, :], scalar=pcol("norm_final", k),
                                       in1=nrs[:, :], op0=ALU.mult, op1=ALU.mult).then_inc(n_t, 1)


_INS = ["x_prompt", "x_sample", "state_gla", "state_rwkv", "state_rwkv_shift", "cache_ffn_conv",
        "norm_mix", "w_in", "gla_gate_w2", "gla_gate_b", "gla_norm_w", "rwkv_mu", "rwkv_w0", "rwkv_w2",
        "rwkv_a0", "rwkv_a2", "rwkv_g2", "rwkv_k_k", "rwkv_k_a", "rwkv_r_k", "rwkv_ln_w", "rwkv_ln_b",
        "w_out", "norm_ffn", "ffn_w_up", "ffn_conv_w", "ffn_conv_b", "ffn_w_down", "norm_final"]
_STATES = [(DEPTH, 1, GH, GDK, GDV), (DEPTH, 1, RC // RN, RN, RN), (DEPTH, 1, RWKV_COLS), (DEPTH, 1, 2, F)]
_OUTS = [(1, SEQ, D), (1, DEC, D)] + _STATES + _STATES


def kernel(**inputs):
    import numpy as np
    import concourse.bacc as bacc
    from concourse.bass_utils import run_bass_kernel_spmd as run

    nc = bacc.Bacc("TRN2", target_bir_lowering=False, num_devices=1)
    arrays, args = {}, []
    for name in _INS:
        a = np.ascontiguousarray(inputs[name])
        arrays[f"in_{name}"] = a
        args.append(nc.dram_tensor(f"in_{name}", a.shape, mybir.dt.from_np(a.dtype), kind="ExternalInput").ap())
    for i, shape in enumerate(_OUTS):
        args.append(nc.dram_tensor(f"out_{i}", shape, F32, kind="ExternalOutput").ap())
    program(nc, *args)
    r = run(nc, [arrays], core_ids=[0])
    return tuple(r.results[0][f"out_{i}"] for i in range(len(_OUTS)))
```
